# Optimizing a Trainium2 kernel written in Bass

```python
import math
import jax, jax.numpy as jnp
from jax import lax
import numpy as np

D_MODEL = 1024
BATCH = 1
SEQ = 2048
DEPTH = 1

HEAD_DIM = 64
D_DIFF = D_MODEL // 2
D_DIL = D_MODEL - D_DIFF
DIFF_V_DIM = 2 * HEAD_DIM
N_HEADS_DIFF = D_DIFF // DIFF_V_DIM
N_HEADS_DIL = D_DIL // HEAD_DIM
D_MIX = D_DIFF + D_DIL
D_IN = 3 * D_DIFF + 3 * D_DIL
DIL_PATTERNS = ((128, 1), (512, 4), (2048, 16))
DIL_BLOCK = 64
Q_BLOCK = 128
D_FF = 4 * D_MODEL
D_PLE = 256
ROPE_THETA = 10000.0
NORM_EPS = 1e-6
SUBLN_EPS = 1e-5
NEG_INF = -1e30

kernel_name = "hybrid_diffattn_dilated_encoder_layer"

def rms_norm(x, g, eps=NORM_EPS):
    xf = x.astype(jnp.float32)
    y = xf * lax.rsqrt(jnp.mean(xf * xf, axis=-1, keepdims=True) + eps)
    return (y * g.astype(jnp.float32)).astype(x.dtype)

def rope_tables(seq):
    inv = ROPE_THETA ** (-jnp.arange(0, HEAD_DIM, 2, dtype=jnp.float32) / HEAD_DIM)
    ang = jnp.arange(seq, dtype=jnp.float32)[:, None] * inv[None, :]
    return jnp.cos(ang), jnp.sin(ang)

def apply_rope(t, cos, sin):
    t1, t2 = jnp.split(t.astype(jnp.float32), 2, axis=-1)
    out = jnp.concatenate([t1 * cos - t2 * sin, t1 * sin + t2 * cos], axis=-1)
    return out.astype(t.dtype)

def diff_attention(q, k, v, lam, subln_g, lam_init):
    B, H, _, S, Dh = q.shape
    nq = S // Q_BLOCK
    scale = Dh ** -0.5
    qb = q.reshape(B, H, 2, nq, Q_BLOCK, Dh).transpose(3, 0, 1, 2, 4, 5)
    kf = k.astype(jnp.float32)
    vf = v.astype(jnp.float32)

    def block(qblk):
        s = jnp.einsum('bhmqd,bhmkd->bhmqk', qblk.astype(jnp.float32) * scale, kf)
        pr = jax.nn.softmax(s, axis=-1)
        a = pr[:, :, 0] - lam * pr[:, :, 1]
        return jnp.einsum('bhqk,bhkd->bhqd', a, vf)

    o = lax.map(block, qb)
    o = o.transpose(1, 2, 0, 3, 4).reshape(B, H, S, 2 * Dh)
    o = rms_norm(o, subln_g, SUBLN_EPS) * (1.0 - lam_init)
    return o

def dilated_branch(q, k, v, dilation, radius):
    B, H, S, Dh = q.shape
    L = S // dilation

    def split(t):
        return t.reshape(B, H, L, dilation, Dh).transpose(0, 1, 3, 2, 4)

    qs, ks, vs = split(q), split(k), split(v)
    nb = -(-L // DIL_BLOCK)
    Lp = nb * DIL_BLOCK
    qb = jnp.pad(qs, ((0, 0), (0, 0), (0, 0), (0, Lp - L), (0, 0)))
    qb = qb.reshape(B, H, dilation, nb, DIL_BLOCK, Dh)

    def windows(t):
        tp = jnp.pad(t, ((0, 0), (0, 0), (0, 0), (DIL_BLOCK, Lp - L + DIL_BLOCK), (0, 0)))
        tb = tp.reshape(B, H, dilation, nb + 2, DIL_BLOCK, Dh)
        return jnp.concatenate([tb[:, :, :, :-2], tb[:, :, :, 1:-1], tb[:, :, :, 2:]], axis=-2)

    kw, vw = windows(ks), windows(vs)
    s = jnp.einsum('bhrnqd,bhrnkd->bhrnqk', qb.astype(jnp.float32),
                   kw.astype(jnp.float32)) * (Dh ** -0.5)
    a = jnp.arange(DIL_BLOCK)[:, None]
    c = jnp.arange(3 * DIL_BLOCK)[None, :]
    off = c - DIL_BLOCK - a
    kpos = (jnp.arange(nb)[:, None, None] - 1) * DIL_BLOCK + c[None]
    mask = (jnp.abs(off)[None] <= radius) & (kpos >= 0) & (kpos < L)
    s = jnp.where(mask, s, NEG_INF)
    lse = jax.nn.logsumexp(s, axis=-1)
    pr = jnp.exp(s - lse[..., None])
    o = jnp.einsum('bhrnqk,bhrnkd->bhrnqd', pr, vw.astype(jnp.float32))
    o = o.reshape(B, H, dilation, Lp, Dh)[:, :, :, :L]
    lse = lse.reshape(B, H, dilation, Lp)[:, :, :, :L]
    o = o.transpose(0, 1, 3, 2, 4).reshape(B, H, S, Dh)
    lse = lse.transpose(0, 1, 3, 2).reshape(B, H, S)
    return o, lse

def dilated_attention(q, k, v):
    outs, lses = [], []
    for window, dilation in DIL_PATTERNS:
        o, l = dilated_branch(q, k, v, dilation, window // (2 * dilation))
        outs.append(o)
        lses.append(l)
    w = jax.nn.softmax(jnp.stack(lses, axis=0), axis=0)
    return jnp.sum(w[..., None] * jnp.stack(outs, axis=0), axis=0)

def setup_inputs(seed: int = 0) -> dict:
    key = jax.random.key(seed)
    ks = jax.random.split(key, 20)
    f32 = jnp.float32
    nrm = lambda k, shape, s: jax.random.normal(k, shape, f32) * s
    gain = lambda k, shape: 1.0 + 0.05 * jax.random.normal(k, shape, f32)
    return {
        "x": jax.random.normal(ks[0], (BATCH, SEQ, D_MODEL), f32),
        "p": jax.random.normal(ks[1], (DEPTH, BATCH, SEQ, D_PLE), f32),
        "w_in": nrm(ks[2], (DEPTH, D_MODEL, D_IN), D_MODEL ** -0.5),
        "w_out": nrm(ks[3], (DEPTH, D_MIX, D_MODEL), D_MIX ** -0.5),
        "g_mix": gain(ks[4], (DEPTH, D_MODEL)),
        "lambda_q1": nrm(ks[5], (DEPTH, HEAD_DIM), 0.1),
        "lambda_k1": nrm(ks[6], (DEPTH, HEAD_DIM), 0.1),
        "lambda_q2": nrm(ks[7], (DEPTH, HEAD_DIM), 0.1),
        "lambda_k2": nrm(ks[8], (DEPTH, HEAD_DIM), 0.1),
        "g_subln": gain(ks[9], (DEPTH, DIFF_V_DIM)),
        "g_mlp": gain(ks[10], (DEPTH, D_MODEL)),
        "w_up": nrm(ks[11], (DEPTH, D_MODEL, D_FF), D_MODEL ** -0.5),
        "w_down": nrm(ks[12], (DEPTH, D_FF, D_MODEL), 0.5 * D_FF ** -0.5),
        "g_ple": gain(ks[13], (DEPTH, D_MODEL)),
        "w_ple_gate": nrm(ks[14], (DEPTH, D_MODEL, D_MODEL), D_MODEL ** -0.5),
        "w_ple_proj": nrm(ks[15], (DEPTH, D_PLE, D_MODEL), D_PLE ** -0.5),
        "g_final": gain(ks[16], (D_MODEL,)),
    }

def reference(x, p, w_in, w_out, g_mix, lambda_q1, lambda_k1, lambda_q2, lambda_k2, g_subln,
              g_mlp, w_up, w_down, g_ple, w_ple_gate, w_ple_proj, g_final):
    B, S, _ = x.shape
    cos, sin = rope_tables(S)
    splits = [D_DIFF, 2 * D_DIFF, 3 * D_DIFF, 3 * D_DIFF + D_DIL, 3 * D_DIFF + 2 * D_DIL]
    h = x
    for i in range(DEPTH):
        hn = rms_norm(h, g_mix[i])
        proj = hn @ w_in[i]
        qd, kd, vd, qg, kg, vg = jnp.split(proj, splits, axis=-1)

        qd = apply_rope(qd.reshape(B, S, N_HEADS_DIFF, 2, HEAD_DIM).transpose(0, 2, 3, 1, 4), cos, sin)
        kd = apply_rope(kd.reshape(B, S, N_HEADS_DIFF, 2, HEAD_DIM).transpose(0, 2, 3, 1, 4), cos, sin)
        vd = vd.reshape(B, S, N_HEADS_DIFF, DIFF_V_DIM).transpose(0, 2, 1, 3)
        lam_init = 0.8 - 0.6 * math.exp(-0.3 * i)
        lam = (jnp.exp(jnp.sum(lambda_q1[i].astype(jnp.float32) * lambda_k1[i].astype(jnp.float32)))
               - jnp.exp(jnp.sum(lambda_q2[i].astype(jnp.float32) * lambda_k2[i].astype(jnp.float32)))
               + lam_init)
        od = diff_attention(qd, kd, vd, lam, g_subln[i], lam_init)
        od = od.transpose(0, 2, 1, 3).reshape(B, S, D_DIFF)

        qg = apply_rope(qg.reshape(B, S, N_HEADS_DIL, HEAD_DIM).transpose(0, 2, 1, 3), cos, sin)
        kg = apply_rope(kg.reshape(B, S, N_HEADS_DIL, HEAD_DIM).transpose(0, 2, 1, 3), cos, sin)
        vg = vg.reshape(B, S, N_HEADS_DIL, HEAD_DIM).transpose(0, 2, 1, 3)
        og = dilated_attention(qg, kg, vg)
        og = og.transpose(0, 2, 1, 3).reshape(B, S, D_DIL)

        mixed = jnp.concatenate([od, og], axis=-1).astype(h.dtype)
        h = h + mixed @ w_out[i]

        hn = rms_norm(h, g_mlp[i])
        h = h + jnp.square(jax.nn.relu(hn @ w_up[i])) @ w_down[i]

        gate = jax.nn.sigmoid(rms_norm(h, g_ple[i]) @ w_ple_gate[i])
        h = h + gate * (p[i] @ w_ple_proj[i])
    return rms_norm(h, g_final)


_drawn_inputs = setup_inputs


def setup_inputs(seed=0):
    import zlib

    import numpy as np

    out = dict(_drawn_inputs(seed))
    spreads = {}
    factors = {'lambda_q1': 8.0, 'lambda_k2': 3.149, 'g_ple': 7.338}
    for name, (base, spread) in spreads.items():
        noise = np.random.default_rng([zlib.crc32(name.encode()), seed]).standard_normal(out[name].shape)
        drawn = base * np.exp(spread * noise) if base else spread * noise
        out[name] = __import__('jax').numpy.asarray(drawn.astype(out[name].dtype))
    for name, factor in factors.items():
        out[name] = (out[name] * factor).astype(out[name].dtype)
    return out
```

```python
from contextlib import ExitStack

import numpy as np
import concourse.bass as bass
from concourse import mybir

P = 128
SEQ = 2048
DM = 1024
TILES = SEQ // P
PAIRS = TILES // 2
KC = DM // P
HD = 64
GROUP = 512
MAPS = GROUP // HD
D_FF = 4 * DM
D_PLE = 256
NORM_EPS = 1e-6
SUBLN_EPS = 1e-5
SCALE = HD ** -0.5
NEG = -1e30
PATTERNS = ((128, 1), (512, 4), (2048, 16))
RADIUS = 64
LAM_INIT = 0.8 - 0.6 * 1.0
START = 24

ALU = mybir.AluOpType
ACT = mybir.ActivationFunctionType
F32 = mybir.dt.float32
F32R = mybir.dt.float32r
AX = mybir.AxisListType


class Kit:

    def __init__(self, nc, dram):
        self.nc, self.dram, self.sems = nc, dram, []

    def sem(self, name):
        self.sems.append(self.nc.alloc_semaphore(name=name))
        return self.sems[-1]

    def sem_pair(self, name):
        return [self.sem(f"{name}{i}") for i in range(2)]


class Tile:

    def __init__(self, q, j, s):
        self.q, self.j, self.s = q, j, s
        self.n = q * 2 + s
        self.t = j * 2 + s

    def next(self, k):
        s = (self.s + k) % 2
        up = 1 if self.s + k >= 2 else 0
        j = self.j + up
        if isinstance(j, int) and j == PAIRS:
            j = 0
        return Tile(self.q + up, j, s)

    def before(self):
        return Tile(self.q, self.j, 0) if self.s else Tile(self.q - 1, self.j - 1, 1)


def matmul3(nc, out, lhs_hi, lhs_lo, rhs_hi, rhs_lo, first, last):
    nc.tensor.matmul(out, lhs_hi, rhs_hi, start=first, stop=False)
    nc.tensor.matmul(out, lhs_hi, rhs_lo, start=False, stop=False)
    return nc.tensor.matmul(out, lhs_lo, rhs_hi, start=False, stop=last)


def project_phase(kit):
    nc, D = kit.nc, kit.dram
    KINDS, G = 2, 3
    with ExitStack() as mem:
        sb = lambda name, shape, dt=F32: mem.enter_context(nc.sbuf_tensor("a_" + name, shape, dt))
        ps = lambda name, shape: mem.enter_context(nc.psum_tensor("a_" + name, shape, F32))
        w_raw = sb("w_raw", [P, 2, KC, GROUP])
        w_hi = sb("w_hi", [P, G, KC, GROUP], F32R)
        w_lo = sb("w_lo", [P, G, KC, GROUP], F32R)
        gain = sb("gain", [P, DM])
        ident = sb("ident", [P, P])
        x = sb("x", [P, 2, DM])
        rot = sb("rot", [P, 2, 2, HD])
        xn = sb("xn", [P, 2, DM])
        junk = sb("junk", [P, DM])
        ssq = sb("ssq", [P, 2])
        mean = sb("mean", [P, 2])
        rstd = sb("rstd", [P, 2])
        half = sb("half", [P, 1])
        xt_hi = sb("xt_hi", [P, 2, KC, P], F32R)
        xt_lo = sb("xt_lo", [P, 2, KC, P], F32R)
        raw = sb("raw", [P, 2, GROUP])
        t_cos = sb("t_cos", [P, 2, GROUP])
        t_sin = sb("t_sin", [P, 2, GROUP])
        out = sb("out", [P, 2, 2, GROUP])
        v_out = sb("v_out", [P, 2, 2, GROUP], F32R)
        turned = ps("turned", [P, 2, 4 * P])
        acc = ps("acc", [P, 2, G, GROUP])

        const_in, half_set = kit.sem("a_const_in"), kit.sem("a_half_set")
        w_in, x_in, rot_in, stored = (kit.sem_pair("a_" + s) for s in ("w_in", "x_in", "rot_in", "stored"))
        w_hi_done, w_lo_done, w_used = kit.sem("a_w_hi"), kit.sem("a_w_lo"), kit.sem("a_w_used")
        ssq_done, mean_done, rstd_done, xn_done = (kit.sem("a_" + s) for s in ("ssq", "mean", "rstd", "xn"))
        turned_done, hi_done, lo_done = (kit.sem("a_" + s) for s in ("turned", "hi", "lo"))
        acc_done, acc_out = kit.sem("a_acc"), kit.sem("a_acc_out")
        v_lo_done = kit.sem("a_v_lo")
        cos_done, sin_done, rope_done = (kit.sem("a_" + s) for s in ("cos", "sin", "rope"))
        STORES = 6 * 16

        def passes(eng, pair, between):
            for kind in range(KINDS):
                with eng.Fori(0, PAIRS - 1) as i:
                    pair(kind, i + kind * PAIRS, i, False)
                pair(kind, kind * PAIRS + PAIRS - 1, PAIRS - 1, kind == KINDS - 1)
                between(kind)

        with nc.Block() as block:

            @block.sync
            def _(sp):
                def load_w(n):
                    if n >= 2:
                        sp.wait_ge(w_lo_done, n - 1 + START)
                    sp.dma_start(w_raw[:, n % 2], D["w_in"][:, n * GROUP:(n + 1) * GROUP].rearrange(
                        "(c p) n -> p c n", p=P)).then_inc(w_in[n % 2], 16)

                def load_x(a):
                    sp.wait_ge(xn_done, a.n - 1 + START)
                    sp.dma_start(x[:, a.s], D["x"][bass.ts(a.t, P), :]).then_inc(x_in[a.s], 16)

                def load_rot(a):
                    sp.wait_ge(rope_done, a.n * 2 - 2 + START)
                    sp.dma_start(rot[:, a.s], D["rot"][bass.ts(a.t, P)]).then_inc(rot_in[a.s], 16)

                def store(kind, a):
                    for g in range(2):
                        sp.wait_ge(rope_done, a.n * 2 + (g + 1 + START))
                        for dup in range(2):
                            sp.dma_start(D["qk"][kind, g, bass.ts(a.t, P), :, dup],
                                         out[:, a.s, g].rearrange("p (m d) -> p m d", d=HD)).then_inc(stored[a.s], 16)
                    sp.wait_ge(v_lo_done, a.n + (1 + START))
                    d = (P, HD)[kind]
                    for u in range(2):
                        sp.dma_start(D["v"][kind, bass.ts(a.t, P)].rearrange("p (h u d) -> p h u d", u=2, d=d)[:, :, u],
                                     v_out[:, a.s, u].bitcast(F32).rearrange("p (h d) -> p h d", d=d)
                                     ).then_inc(stored[a.s], 16)

                for s in range(2):
                    sp.sem_inc(stored[s], STORES)
                sp.dma_start(gain[:], D["g_mix"].partition_broadcast(P)).then_inc(const_in, 16)
                sp.dma_start(ident[:], D["ident"][:]).then_inc(const_in, 16)
                load_x(Tile(0, 0, 0))
                load_w(0)
                load_x(Tile(0, 0, 1))
                load_rot(Tile(0, 0, 0))
                for n in range(1, G + 2):
                    load_w(n)

                def pair(kind, q, j, last):
                    for s in range(2):
                        a = Tile(q, j, s)
                        if not last:
                            load_x(a.next(2))
                        if not (last and s == 1):
                            load_rot(a.next(1))
                        store(kind, a)

                passes(sp, pair, lambda kind: load_w(G + 2) if kind == 0 else None)
                for s in range(2):
                    sp.wait_ge(stored[s], STORES * (KINDS * PAIRS + 1))

            @block.scalar
            def _(act):
                def split_w(n):
                    act.wait_ge(w_in[n % 2], 16 * (n // 2 + 1))
                    if n >= G:
                        act.wait_ge(acc_done, (TILES - 1) * G + n - G + 1 + START)
                    nc.scalar.copy(w_hi[:, n % G], w_raw[:, n % 2]).then_inc(w_hi_done, 1)

                def square(a):
                    act.wait_ge(x_in[a.s], a.q * 16 + 16)
                    act.wait_ge(ssq_done, a.n + START)
                    nc.scalar.activation(junk[:], x[:, a.s], ACT.Square,
                                         accum_out=ssq[:, a.s:a.s + 1]).then_inc(ssq_done, 1)

                def hi(a):
                    act.wait_ge(acc_done, a.n * 3 - 3 + START)
                    for b in range(2):
                        act.wait_ge(turned_done, a.n * 2 + (b + 1 + START))
                        nc.scalar.copy(xt_hi[:, a.s, 4 * b:4 * b + 4].rearrange("p c t -> p (c t)"),
                                       turned[:, b]).then_inc(hi_done, 1)

                def evacuate(a):
                    for g in range(2):
                        act.wait_ge(acc_done, a.n * 3 + (g + 1 + START))
                        act.wait_ge(rope_done, a.n * 2 + (g - 1 + START))
                        nc.scalar.copy(raw[:, g], acc[:, a.s, g]).then_inc(acc_out, 1)
                    act.wait_ge(acc_done, a.n * 3 + (3 + START))
                    act.wait_ge(stored[a.s], a.q * STORES + STORES)
                    nc.scalar.copy(v_out[:, a.s, 0], acc[:, a.s, 2]).then_inc(acc_out, 1)

                def pair(kind, q, j, last):
                    for s in range(2):
                        a = Tile(q, j, s)
                        if not (last and s == 1):
                            hi(a.next(1))
                        if not last:
                            square(a.next(2))
                        evacuate(a)

                for step in (ssq_done, hi_done, w_hi_done, acc_out):
                    act.sem_inc(step, START)
                square(Tile(0, 0, 0))
                square(Tile(0, 0, 1))
                split_w(0)
                hi(Tile(0, 0, 0))
                split_w(1)
                split_w(2)
                passes(act, pair, lambda kind: [split_w(n) for n in range(G, 2 * G)] if kind == 0 else None)

            @block.vector
            def _(dve):
                def split_w(n):
                    dve.wait_ge(w_hi_done, n + 1 + START)
                    nc.vector.tensor_tensor(w_lo[:, n % G], w_raw[:, n % 2], w_hi[:, n % G].bitcast(F32),
                                            ALU.subtract).then_inc(w_lo_done, 1)

                def normalise(a):
                    v = slice(a.s, a.s + 1)
                    dve.wait_ge(ssq_done, a.n + (1 + START))
                    nc.vector.tensor_scalar(mean[:, v], ssq[:, v], 1.0 / DM, NORM_EPS,
                                            ALU.mult, ALU.add).then_inc(mean_done, 1)
                    dve.wait_ge(rstd_done, a.n + (1 + START))
                    dve.wait_ge(turned_done, a.n * 2 + (START - 2))
                    nc.vector.scalar_tensor_tensor(out=xn[:, a.s], in0=x[:, a.s], scalar=rstd[:, v], in1=gain[:],
                                                   op0=ALU.mult, op1=ALU.mult).then_inc(xn_done, 1)

                def lo(a):
                    for b in range(2):
                        dve.wait_ge(hi_done, a.n * 2 + (b + 1 + START))
                        nc.vector.tensor_tensor(
                            xt_lo[:, a.s, 4 * b:4 * b + 4].rearrange("p c t -> p (c t)"), turned[:, b],
                            xt_hi[:, a.s, 4 * b:4 * b + 4].rearrange("p c t -> p (c t)").bitcast(F32),
                            ALU.subtract).then_inc(lo_done, 1)

                def rotate(a):
                    dve.wait_ge(rot_in[a.s], a.q * 16 + 16)
                    for g in range(2):
                        view = lambda t: t.rearrange("p (m d) -> p m d", d=HD)
                        dve.wait_ge(acc_out, a.n * 3 + (g + 1 + START))
                        nc.vector.tensor_tensor(view(t_cos[:, g]), view(raw[:, g]),
                                                rot[:, a.s, 0].unsqueeze(1).to_broadcast([P, MAPS, HD]),
                                                ALU.mult).then_inc(cos_done, 1)
                        dve.wait_ge(cos_done, a.n * 2 + (g + 1 + START))
                        dve.wait_ge(sin_done, a.n * 4 + (2 * g + 2 + START))
                        dve.wait_ge(stored[a.s], a.q * STORES + STORES)
                        nc.vector.tensor_tensor(out[:, a.s, g], t_cos[:, g], t_sin[:, g],
                                                ALU.add).then_inc(rope_done, 1)

                def split_v(a):
                    dve.wait_ge(acc_out, a.n * 3 + (3 + START))
                    nc.vector.tensor_tensor(v_out[:, a.s, 1], acc[:, a.s, 2], v_out[:, a.s, 0].bitcast(F32),
                                            ALU.subtract).then_inc(v_lo_done, 1)

                for step in (mean_done, xn_done, w_lo_done, lo_done, cos_done, rope_done, v_lo_done):
                    dve.sem_inc(step, START)
                dve.wait_ge(const_in, 32)
                normalise(Tile(0, 0, 0))
                normalise(Tile(0, 0, 1))
                split_w(0)
                lo(Tile(0, 0, 0))
                split_w(1)
                split_w(2)

                def pair(kind, q, j, last):
                    for s in range(2):
                        a = Tile(q, j, s)
                        if not (last and s == 1):
                            lo(a.next(1))
                        if not last:
                            normalise(a.next(2))
                        rotate(a)
                        split_v(a)

                passes(dve, pair, lambda kind: [split_w(n) for n in range(G, 2 * G)] if kind == 0 else None)

            @block.gpsimd
            def _(pool):
                def rotate(a):
                    pool.wait_ge(rot_in[a.s], a.q * 16 + 16)
                    for g in range(2):
                        pool.wait_ge(acc_out, a.n * 3 + (g + 1 + START))
                        pool.wait_ge(rope_done, a.n * 2 + (g - 1 + START))
                        half = lambda t, h: t.rearrange("p (m h d) -> p m h d", h=2, d=HD // 2)[:, :, h]
                        for h in range(2):
                            nc.gpsimd.tensor_tensor(
                                half(t_sin[:, g], h), half(raw[:, g], 1 - h),
                                rot[:, a.s, 1, h * 32:h * 32 + 32].unsqueeze(1).to_broadcast([P, MAPS, HD // 2]),
                                ALU.mult).then_inc(sin_done, 1)

                def root(a):
                    v = slice(a.s, a.s + 1)
                    pool.wait_ge(mean_done, a.n + (1 + START))
                    nc.gpsimd.tensor_tensor(rstd[:, v], mean[:, v], half[:], ALU.pow).then_inc(rstd_done, 1)

                def pair(kind, q, j, last):
                    for s in range(2):
                        a = Tile(q, j, s)
                        if not last:
                            root(a.next(2))
                        rotate(a)

                for step in (rstd_done, sin_done):
                    pool.sem_inc(step, START)
                nc.gpsimd.memset(half[:], -0.5).then_inc(half_set, 1)
                pool.wait_ge(half_set, 1)
                root(Tile(0, 0, 0))
                root(Tile(0, 0, 1))
                passes(pool, pair, lambda kind: None)

            @block.tensor
            def _(pe):
                def turn(a):
                    pe.wait_ge(xn_done, a.n + (1 + START))
                    for b in range(2):
                        pe.wait_ge(lo_done, a.n * 2 + (b - 1 + START))
                        for c in range(4):
                            ins = nc.tensor.transpose(turned[:, b, c * P:(c + 1) * P],
                                                      xn[:, a.s, (4 * b + c) * P:(4 * b + c + 1) * P], ident[:])
                        ins.then_inc(turned_done, 1)

                def project(kind, a):
                    pe.wait_ge(lo_done, a.n * 2 + (2 + START))
                    for g in range(G):
                        pe.wait_ge(w_lo_done, kind * G + g + 1 + START)
                        if g == 2:
                            pe.wait_ge(v_lo_done, a.n - 1 + START)
                        else:
                            pe.wait_ge(acc_out, a.n * 3 + (g - 5 + START))
                        for c in range(KC):
                            ins = matmul3(nc, acc[:, a.s, g], xt_hi[:, a.s, c], xt_lo[:, a.s, c],
                                          w_hi[:, g, c], w_lo[:, g, c], c == 0, c == KC - 1)
                        ins.then_inc(acc_done, 1)

                def pair(kind, q, j, last):
                    for s in range(2):
                        a = Tile(q, j, s)
                        if not (last and s == 1):
                            turn(a.next(1))
                        project(kind, a)

                for step in (turned_done, acc_done):
                    pe.sem_inc(step, START)
                pe.wait_ge(const_in, 32)
                turn(Tile(0, 0, 0))
                passes(pe, pair, lambda kind: None)


def differential_phase(kit):
    nc, D = kit.nc, kit.dram
    HEADS, VD, KT = MAPS // 2, 2 * HD, SEQ // P
    HALF = SEQ // 2
    with ExitStack() as mem:
        sb = lambda name, shape, dt=F32: mem.enter_context(nc.sbuf_tensor("c_" + name, shape, dt))
        ps = lambda name, shape: mem.enter_context(nc.psum_tensor("c_" + name, shape, F32))
        ident = sb("ident", [P, P])
        lam_in = sb("lam_in", [P, 4, HD])
        lam_prod = sb("lam_prod", [P, 2, HD])
        lam_dot = sb("lam_dot", [P, 2])
        lam_exp = sb("lam_exp", [P, 2])
        neg_lam = sb("neg_lam", [P, 1])
        gain_in = sb("gain_in", [P, VD])
        gain = sb("gain", [P, VD])
        half = sb("half", [P, 1])
        k_raw = sb("k_raw", [P, KT, 2, P])
        kt_hi = sb("kt_hi", [P, 2, SEQ], F32R)
        kt_lo = sb("kt_lo", [P, 2, SEQ], F32R)
        v_hl = sb("v_hl", [P, KT, 2, VD], F32R)
        q_raw = sb("q_raw", [P, 2, 2, P])
        qs = sb("qs", [P, 2, 2, P], F32R)
        mx = sb("mx", [P, 2])
        neg_max = sb("neg_max", [P, 2, 2])
        e = sb("e", [P, 2, 2, SEQ])
        sums = sb("sums", [P, 2, 2, 2])
        den = sb("den", [P, 2])
        rec = sb("rec", [P, 2, 2])
        coef = sb("coef", [P, 1])
        a_row = sb("a_row", [P, 2, SEQ])
        at_hi = sb("at_hi", [P, 2, KT, P], F32R)
        at_lo = sb("at_lo", [P, 2, KT, P], F32R)
        o_part = sb("o_part", [P, VD])
        o = sb("o", [P, VD])
        o_junk = sb("o_junk", [P, VD])
        o_ssq = sb("o_ssq", [P, 1])
        o_part_mean = sb("o_part_mean", [P, 1])
        o_mean = sb("o_mean", [P, 1])
        inv_dim, eps = sb("inv_dim", [P, 1]), sb("eps", [P, 1])
        o_rstd = sb("o_rstd", [P, 1])
        o_unit = sb("o_unit", [P, VD])
        out = sb("out", [P, 2, VD])
        scores = ps("scores", [P, 4, 512])
        turned = ps("turned", [P, 2, 512])
        pv = ps("pv", [P, 512])
        q_turned = ps("q_turned", [P, 512])

        const_in, consts, gain_done = kit.sem("c_const_in"), kit.sem("c_consts"), kit.sem("c_gain")
        lam_dots, half_set = kit.sem("c_lam_dots"), kit.sem("c_half_set")
        loads_begun = kit.sem("c_loads_begun")
        k_in, v_in, q_in, stored = kit.sem("c_k_in"), kit.sem("c_v_in"), kit.sem_pair("c_q_in"), kit.sem_pair("c_stored")
        names = ("kt_turned k_hi k_lo q_turn q_hi q_lo scored mx negmax exp den rec coef a a_turned "
                 "a_hi a_lo pv part o ssq scaled mean rstd unit out")
        S = {name: kit.sem("c_" + name) for name in names.split()}

        def steps(eng, head_start, step, head_end):
            with eng.Fori(0, HEADS) as h:
                base = h * TILES
                head_start(h)
                step(h, base, 0, 0, True, 2)
                with eng.Fori(0, PAIRS - 2) as i:
                    step(h, base + (i * 2 + 1), i * 2 + 1, 1, False, 2)
                    step(h, base + (i * 2 + 2), i * 2 + 2, 0, False, 2)
                for t in range(TILES - 3, TILES):
                    step(h, base + t, t, t % 2, False, min(2, TILES - 1 - t))
                head_end(h, base + (TILES - 1))

        with nc.Block() as block:

            @block.sync
            def _(sp):
                def load_q(h, n, t, s):
                    sp.wait_ge(S["q_turn"], n - 1 + START)
                    sp.sem_inc(loads_begun, 1)
                    sp.dma_start(q_raw[:, s], D["qk"][0, 0, bass.ts(t, P), bass.ts(h, 2)].rearrange(
                        "p m u d -> p m (u d)")).then_inc(q_in[s], 16)

                def head_start(h):
                    sp.wait_ge(S["kt_turned"], h * 8 + START)
                    sp.sem_inc(loads_begun, 1)
                    sp.dma_start(k_raw[:], D["qk"][0, 1, :, bass.ts(h, 2)].rearrange(
                        "(t p) m u d -> p t m (u d)", p=P)).then_inc(k_in, 16)
                    sp.wait_ge(S["pv"], h * TILES + START)
                    sp.sem_inc(loads_begun, 1)
                    sp.dma_start(v_hl[:].rearrange("p t u d -> p t (u d)").bitcast(F32),
                                 D["v"][0, :, bass.ts(h, 2 * VD)].rearrange("(t p) d -> p t d", p=P)).then_inc(v_in, 16)
                    load_q(h, h * TILES, 0, 0)
                    load_q(h, h * TILES + 1, 1, 1)
                    load_q(h, h * TILES + 2, 2, 0)

                def store(h, n, t, s):
                    sp.wait_ge(S["out"], n + (1 + START))
                    sp.dma_start(D["od"][bass.ts(t, P), bass.ts(h, VD)], out[:, s]).then_inc(stored[s], 16)

                def step(h, n, t, s, first, more):
                    if not isinstance(t, int) or t <= TILES - 4:
                        load_q(h, n + 3, t + 3, 1 - s)
                    if not first:
                        store(h, n - 1, t - 1, 1 - s)

                for s in range(2):
                    sp.sem_inc(stored[s], 16)

                sp.dma_start(ident[:], D["ident"][:]).then_inc(const_in, 16)
                for k, name in enumerate(("lambda_q1", "lambda_k1", "lambda_q2", "lambda_k2")):
                    sp.dma_start(lam_in[:, k], D[name][0].partition_broadcast(P)).then_inc(const_in, 16)
                sp.dma_start(gain_in[:], D["g_subln"].partition_broadcast(P)).then_inc(const_in, 16)
                steps(sp, head_start, step, lambda h, n: store(h, n, TILES - 1, 1))
                for s in range(2):
                    sp.wait_ge(stored[s], 16 * (HEADS * PAIRS + 1))

            @block.scalar
            def _(act):
                def q_hi(n, s):
                    act.wait_ge(S["q_turn"], n + (1 + START))
                    nc.scalar.copy(qs[:, s].rearrange("p m t -> p (m t)"), q_turned[:, :2 * P]).then_inc(S["q_hi"], 1)

                def exp(n, s, m, f):
                    act.wait_ge(S["negmax"], n * 2 + (m + 1 + START))
                    if m == 0 and f == 0:
                        act.wait_ge(S["a"], n - 1 + START)
                    nc.scalar.activation(e[:, s, m, f * HALF:(f + 1) * HALF],
                                         scores[:, 2 * f:2 * f + 2].rearrange("p b k -> p (b k)"), ACT.Exp,
                                         bias=neg_max[:, s, m:m + 1], scale=SCALE,
                                         accum_out=sums[:, s, m, f:f + 1]).then_inc(S["exp"], 1)

                def a_hi(n, s, g):
                    act.wait_ge(S["a_turned"], n * 4 + (g + 1 + START))
                    nc.scalar.copy(at_hi[:, s, 4 * g:4 * g + 4].rearrange("p c t -> p (c t)"),
                                   turned[:, g % 2]).then_inc(S["a_hi"], 1)

                def part(n, s):
                    act.wait_ge(S["pv"], n + (1 + START))
                    act.wait_ge(S["o"], n + START)
                    nc.scalar.activation(o_part[:], pv[:, VD:2 * VD], ACT.Copy,
                                         scale=rec[:, s, 0:1]).then_inc(S["part"], 1)

                def square(n):
                    act.wait_ge(S["o"], n + (1 + START))
                    act.wait_ge(S["ssq"], n + START)
                    nc.scalar.activation(o_junk[:], o[:], ACT.Square, accum_out=o_ssq[:]).then_inc(S["ssq"], 1)

                def unit(n):
                    act.wait_ge(S["rstd"], n + (1 + START))
                    act.wait_ge(S["out"], n + START)
                    nc.scalar.activation(o_unit[:], o[:], ACT.Copy, scale=o_rstd[:]).then_inc(S["unit"], 1)

                def head_start(h):
                    for g in range(8):
                        act.wait_ge(S["kt_turned"], h * 8 + (g + 1 + START))
                        nc.scalar.copy(kt_hi[:, g // 4, (g % 4) * 512:(g % 4) * 512 + 512],
                                       scores[:, g % 4]).then_inc(S["k_hi"], 1)
                    q_hi(h * TILES, 0)
                    for m in range(2):
                        if m == 1:
                            q_hi(h * TILES + 1, 1)
                        for f in range(2):
                            exp(h * TILES, 0, m, f)

                def step(h, n, t, s, first, more):
                    if more:
                        exp(n + 1, 1 - s, 0, 0)
                        exp(n + 1, 1 - s, 0, 1)
                    if not first:
                        part(n - 1, 1 - s)
                    if more == 2:
                        q_hi(n + 2, s)
                    a_hi(n, s, 0)
                    a_hi(n, s, 1)
                    if more:
                        exp(n + 1, 1 - s, 1, 0)
                    a_hi(n, s, 2)
                    if more:
                        exp(n + 1, 1 - s, 1, 1)
                    a_hi(n, s, 3)
                    if not first:
                        square(n - 1)
                        unit(n - 1)

                def head_end(h, n):
                    part(n, 1)
                    square(n)
                    unit(n)

                for name in "k_hi q_hi exp a_hi part ssq unit".split():
                    act.sem_inc(S[name], START)
                act.wait_ge(consts, 1)
                nc.scalar.activation(lam_exp[:], lam_dot[:], ACT.Exp).then_inc(consts, 1)
                act.wait_ge(const_in, 96)
                nc.scalar.mul(gain[:], gain_in[:], 1.0 - LAM_INIT).then_inc(gain_done, 1)
                steps(act, head_start, step, head_end)

            @block.vector
            def _(dve):
                def q_lo(n, s):
                    dve.wait_ge(S["q_hi"], n + (1 + START))
                    low = qs[HD:, s].rearrange("p m t -> p (m t)")
                    nc.vector.tensor_tensor(low, q_turned[HD:, :2 * P], low.bitcast(F32),
                                            ALU.subtract).then_inc(S["q_lo"], 1)

                def maximum(n, s, m):
                    for f in range(2):
                        dve.wait_ge(S["scored"], n * 4 + (2 * m + f + 1 + START))
                        dve.wait_ge(S["negmax"], n * 2 + (m + START))
                        nc.vector.tensor_reduce(mx[:, f:f + 1], scores[:, 2 * f:2 * f + 2].rearrange("p b k -> p (b k)"),
                                                AX.X, ALU.max).then_inc(S["mx"], 1)
                    dve.wait_ge(S["mx"], n * 4 + (2 * m + 2 + START))
                    nc.vector.tensor_scalar(neg_max[:, s, m:m + 1], mx[:, 0:1], mx[:, 1:2], -SCALE,
                                            ALU.max, ALU.mult).then_inc(S["negmax"], 1)

                def combine(n, s):
                    dve.wait_ge(S["exp"], n * 4 + (4 + START))
                    nc.vector.tensor_tensor(den[:], sums[:, s, :, 0], sums[:, s, :, 1], ALU.add).then_inc(S["den"], 1)
                    dve.wait_ge(S["den"], n + (1 + START))
                    dve.wait_ge(S["part"], n - 1 + START)
                    nc.vector.reciprocal(rec[:, s], den[:]).then_inc(S["rec"], 1)
                    dve.wait_ge(S["rec"], n + (1 + START))
                    nc.vector.tensor_scalar(coef[:], den[:, 0:1], neg_lam[:], rec[:, s, 1:2],
                                            ALU.mult, ALU.mult).then_inc(S["coef"], 1)
                    dve.wait_ge(S["coef"], n + (1 + START))
                    dve.wait_ge(S["a_turned"], n * 4 - 4 + START)
                    nc.vector.scalar_tensor_tensor(out=a_row[:, s], in0=e[:, s, 1], scalar=coef[:], in1=e[:, s, 0],
                                                   op0=ALU.mult, op1=ALU.add).then_inc(S["a"], 1)

                def a_lo(n, s, g):
                    dve.wait_ge(S["a_hi"], n * 4 + (g + 1 + START))
                    view = lambda t: t[:, s, 4 * g:4 * g + 4].rearrange("p c t -> p (c t)")
                    nc.vector.tensor_tensor(view(at_lo), turned[:, g % 2], view(at_hi).bitcast(F32),
                                            ALU.subtract).then_inc(S["a_lo"], 1)

                def result(n, s):
                    dve.wait_ge(S["part"], n + (1 + START))
                    dve.wait_ge(S["unit"], n + START)
                    nc.vector.scalar_tensor_tensor(out=o[:], in0=pv[:, :VD], scalar=rec[:, s, 0:1], in1=o_part[:],
                                                   op0=ALU.mult, op1=ALU.add).then_inc(S["o"], 1)

                def head_start(h):
                    for g in range(8):
                        dve.wait_ge(S["k_hi"], h * 8 + (g + 1 + START))
                        cols = slice((g % 4) * 512, (g % 4) * 512 + 512)
                        nc.vector.tensor_tensor(kt_lo[:, g // 4, cols], scores[:, g % 4],
                                                kt_hi[:, g // 4, cols].bitcast(F32), ALU.subtract).then_inc(S["k_lo"], 1)
                    q_lo(h * TILES, 0)
                    maximum(h * TILES, 0, 0)
                    q_lo(h * TILES + 1, 1)
                    maximum(h * TILES, 0, 1)

                def step(h, n, t, s, first, more):
                    if more:
                        maximum(n + 1, 1 - s, 0)
                    combine(n, s)
                    if more:
                        maximum(n + 1, 1 - s, 1)
                    if more == 2:
                        q_lo(n + 2, s)
                    a_lo(n, s, 0)
                    a_lo(n, s, 1)
                    if not first:
                        result(n - 1, 1 - s)
                    a_lo(n, s, 2)
                    a_lo(n, s, 3)

                for name in "k_lo q_lo mx negmax den rec coef a a_lo o".split():
                    dve.sem_inc(S[name], START)
                dve.wait_ge(const_in, 96)
                for k in range(2):
                    nc.vector.tensor_tensor_reduce(lam_prod[:, k], lam_in[:, 2 * k], lam_in[:, 2 * k + 1], 1.0, 0.0,
                                                   ALU.mult, ALU.add, lam_dot[:, k:k + 1]).then_inc(lam_dots, 1)
                dve.wait_ge(lam_dots, 2)
                dve.sem_inc(consts, 1)
                dve.wait_ge(consts, 2)
                nc.vector.tensor_scalar(neg_lam[:], lam_exp[:, 1:2], lam_exp[:, 0:1], -LAM_INIT,
                                        ALU.subtract, ALU.add).then_inc(consts, 1)
                dve.wait_ge(consts, 3)
                steps(dve, head_start, step, lambda h, n: result(n, 1))

            @block.gpsimd
            def _(pool):
                def finish(n, s):
                    pool.wait_ge(S["ssq"], n + (1 + START))
                    nc.gpsimd.tensor_tensor(o_part_mean[:], o_ssq[:], inv_dim[:], ALU.mult).then_inc(S["scaled"], 1)
                    pool.wait_ge(S["scaled"], n + (1 + START))
                    nc.gpsimd.tensor_tensor(o_mean[:], o_part_mean[:], eps[:], ALU.add).then_inc(S["mean"], 1)
                    pool.wait_ge(S["mean"], n + (1 + START))
                    nc.gpsimd.tensor_tensor(o_rstd[:], o_mean[:], half[:], ALU.pow).then_inc(S["rstd"], 1)
                    pool.wait_ge(S["unit"], n + (1 + START))
                    pool.wait_ge(stored[s], (n - s) * 8 + 16)
                    nc.gpsimd.tensor_tensor(out[:, s], o_unit[:], gain[:], ALU.mult).then_inc(S["out"], 1)

                for name in "scaled mean rstd out".split():
                    pool.sem_inc(S[name], START)
                nc.gpsimd.memset(half[:], -0.5).then_inc(half_set, 1)
                nc.gpsimd.memset(inv_dim[:], 1.0 / VD).then_inc(half_set, 1)
                nc.gpsimd.memset(eps[:], SUBLN_EPS).then_inc(half_set, 1)
                pool.wait_ge(half_set, 3)
                pool.wait_ge(gain_done, 1)
                steps(pool, lambda h: None,
                      lambda h, n, t, s, first, more: None if first else finish(n - 1, 1 - s),
                      lambda h, n: finish(n, 1))

            @block.tensor
            def _(pe):
                def turn_q(n, s):
                    pe.wait_ge(q_in[s], (n - s) * 8 + 16)
                    pe.wait_ge(S["q_lo"], n + START)
                    for m in range(2):
                        ins = nc.tensor.transpose(q_turned[:, m * P:(m + 1) * P], q_raw[:, s, m], ident[:])
                    ins.then_inc(S["q_turn"], 1)

                def score(n, s, m):
                    pe.wait_ge(S["q_lo"], n + (1 + START))
                    for b in range(4):
                        if b % 2 == 0:
                            pe.wait_ge(S["exp"], n * 4 + (2 * m - 2 + b // 2 + 1 + START))
                        cols = slice(b * 512, b * 512 + 512)
                        nc.tensor.matmul(scores[:, b], qs[:, s, m], kt_hi[:, m, cols], start=True, stop=False)
                        ins = nc.tensor.matmul(scores[:, b], qs[:, s, m], kt_lo[:, m, cols], start=False, stop=True)
                        if b % 2 == 1:
                            ins.then_inc(S["scored"], 1)

                def turn_a(n, s, g):
                    pe.wait_ge(S["a"], n + (1 + START))
                    pe.wait_ge(S["a_lo"], n * 4 + (g - 1 + START))
                    for c in range(4):
                        ins = nc.tensor.transpose(turned[:, g % 2, c * P:(c + 1) * P],
                                                  a_row[:, s, (4 * g + c) * P:(4 * g + c + 1) * P], ident[:])
                    ins.then_inc(S["a_turned"], 1)

                def values(h, n, s):
                    pe.wait_ge(S["a_lo"], n * 4 + (4 + START))
                    pe.wait_ge(v_in, h * 16 + 16)
                    pe.wait_ge(S["o"], n + START)
                    for c in range(KT):
                        nc.tensor.matmul(pv[:, :2 * VD], at_hi[:, s, c], v_hl[:, c].rearrange("p u d -> p (u d)"),
                                         start=(c == 0), stop=False)
                        ins = nc.tensor.matmul(pv[:, :2 * VD], at_lo[:, s, c], v_hl[:, c].rearrange("p u d -> p (u d)"),
                                               start=False, stop=(c == KT - 1))
                    ins.then_inc(S["pv"], 1)

                def head_start(h):
                    pe.wait_ge(k_in, h * 16 + 16)
                    for g in range(8):
                        m, b = g // 4, g % 4
                        if g < 4:
                            pe.wait_ge(S["exp"], h * (TILES * 4) + START)
                        else:
                            pe.wait_ge(S["k_lo"], h * 8 + (g - 3 + START))
                        for c in range(4):
                            ins = nc.tensor.transpose(scores[:, b, c * P:(c + 1) * P], k_raw[:, 4 * b + c, m], ident[:])
                        ins.then_inc(S["kt_turned"], 1)
                    turn_q(h * TILES, 0)
                    turn_q(h * TILES + 1, 1)
                    pe.wait_ge(S["k_lo"], h * 8 + (8 + START))
                    score(h * TILES, 0, 0)
                    score(h * TILES, 0, 1)

                def step(h, n, t, s, first, more):
                    if more:
                        score(n + 1, 1 - s, 0)
                    if not first:
                        values(h, n - 1, 1 - s)
                    if more == 2:
                        turn_q(n + 2, s)
                    if more:
                        score(n + 1, 1 - s, 1)
                    for g in range(4):
                        turn_a(n, s, g)

                for name in "kt_turned q_turn scored a_turned pv".split():
                    pe.sem_inc(S[name], START)
                pe.wait_ge(const_in, 96)
                steps(pe, head_start, step, lambda h, n: values(h, n, 1))


def dilated_phase(kit):
    nc, D = kit.nc, kit.dram
    HEADS, NP = MAPS, len(PATTERNS)
    WORK = NP * PAIRS
    EDGE = RADIUS * PATTERNS[1][1]
    KEYS = P + 2 * RADIUS
    SUB = [TILES // d for _, d in PATTERNS]
    CHUNKS = [n + 1 if n > 1 else 1 for n in SUB]
    BASE = [0, CHUNKS[0], CHUNKS[0] + CHUNKS[1] * PATTERNS[1][1]]
    N_CHUNKS = BASE[2] + CHUNKS[2] * PATTERNS[2][1]
    V_LOADS = [16 * (d + 2 if n > 1 else 1) for (_, d), n in zip(PATTERNS, SUB)]
    STORES = [16 * (d if n > 1 else 1) for (_, d), n in zip(PATTERNS, SUB)]
    with ExitStack() as mem:
        sb = lambda name, shape, dt=F32: mem.enter_context(nc.sbuf_tensor("b_" + name, shape, dt))
        ps = lambda name, shape: mem.enter_context(nc.psum_tensor("b_" + name, shape, F32))
        ident = sb("ident", [P, P])
        masks = sb("masks", [P, 4, KEYS])
        raw = sb("raw", [P, 2, TILES, 2 * HD])
        kt = sb("kt", [P, 2, SEQ + 2 * EDGE], F32R)
        qs = sb("qs", [P, SEQ], F32R)
        v_hl = sb("v_hl", [P, N_CHUNKS, 2 * HD], F32R)
        masked = sb("masked", [P, 4, 2, KEYS])
        neg_max = sb("neg_max", [P, 4, 2])
        e = sb("e", [P, 4, 2, KEYS])
        et_hi = sb("et_hi", [P, 2, 4, P], F32R)
        et_lo = sb("et_lo", [P, 2, 4, P], F32R)
        nout = sb("nout", [P, NP, TILES, HD])
        md_head = sb("md_head", [P, NP, TILES, 2])
        md_all = sb("md_all", [P, NP, TILES, HEADS, 2])
        scores = ps("scores", [P, 4, 2, KEYS])
        turned = ps("turned", [P, 2, 4, P])
        pv = ps("pv", [P, 2, 2, 4 * HD])

        const_in, zeroed, raw_in = kit.sem("b_const_in"), kit.sem("b_zeroed"), kit.sem("b_raw_in")
        v_in, stored = ([kit.sem(f"b_{s}{p}") for p in range(NP)] for s in ("v_in", "stored"))
        md_stored = kit.sem("b_md_stored")
        loads_begun, masks_begun = kit.sem("b_loads_begun"), kit.sem("b_masks_begun")
        names = "prep_turn prep_hi prep_lo scored masked negmax exp e_turn e_hi e_lo pv out md"
        S = {name: kit.sem("b_" + name) for name in names.split()}

        def pattern(w):
            return w // PAIRS

        def tile_of(w, s):
            t = w % PAIRS * 2 + s
            return t // SUB[pattern(w)], t % SUB[pattern(w)]

        def used(w, t):
            return t if pattern(w) < 2 else t[:, :, :P]

        def heads(eng, prepare, step):
            with eng.Fori(0, HEADS) as h:
                prepare(h)
                for w in range(WORK + 3):
                    step(h, h * WORK, w)

        with nc.Block() as block:

            @block.sync
            def _(sp):
                def load_raw(h):
                    for g in range(2):
                        sp.dma_start(raw[:, g], D["qk"][1, 1 - g, :, bass.ts(h, 1)].rearrange(
                            "(t p) m u d -> p t (m u d)", p=P)).then_inc(raw_in, 16)

                def load_v(h, p):
                    d, n, b = PATTERNS[p][1], SUB[p], BASE[p]
                    src = D["v"][1, :, bass.ts(h, 2 * HD)].rearrange("(k r) x -> r k x", r=d)
                    dst = v_hl[:, b:b + CHUNKS[p] * d].rearrange("p (r c) x -> p r c x", r=d).bitcast(F32)
                    if n == 1:
                        sp.dma_start(dst[:, :, 0], src.rearrange("r k x -> k r x")).then_inc(v_in[p], 16)
                        return
                    for r in range(d):
                        sp.dma_start(dst[:, r, 1:n], src[r, RADIUS:RADIUS + (n - 1) * P].rearrange(
                            "(c p) x -> p c x", p=P)).then_inc(v_in[p], 16)
                    sp.dma_start(dst[RADIUS:, :, 0], src[:, :RADIUS].rearrange("r k x -> k r x")).then_inc(v_in[p], 16)
                    sp.dma_start(dst[:RADIUS, :, n], src[:, n * P - RADIUS:].rearrange(
                        "r k x -> k r x")).then_inc(v_in[p], 16)

                def by_token(t, p):
                    d, n = PATTERNS[p][1], SUB[p]
                    if n == 1:
                        return [t.rearrange("(k r) x -> k r x", r=d)]
                    return [t.rearrange("(c p r) x -> r p c x", p=P, r=d)[r] for r in range(d)]

                def store(h, p):
                    sp.wait_ge(S["out"], h * WORK + ((p + 1) * PAIRS + START))
                    views = by_token(D["nd"][p].rearrange("s h d -> s (h d)")[:, bass.ts(h, HD)], p)
                    for r, view in enumerate(views):
                        n = TILES // len(views)
                        sp.dma_start(view, nout[:, p, r * n:(r + 1) * n]).then_inc(stored[p], 16)

                for p in range(NP):
                    sp.sem_inc(stored[p], STORES[p])
                sp.dma_start(ident[:], D["ident"][:]).then_inc(const_in, 16)
                load_raw(0)
                sp.dma_start(masks[:], D["masks"][:]).then_inc(const_in, 16)
                for p in range(NP):
                    load_v(0, p)
                with sp.Fori(0, HEADS - 1) as h:
                    sp.wait_ge(S["prep_turn"], h * 8 + (8 + START))
                    sp.sem_inc(loads_begun, 1)
                    load_raw(h + 1)
                    for p in range(NP):
                        store(h, p)
                        sp.wait_ge(S["pv"], h * WORK + ((p + 1) * PAIRS + START))
                        sp.sem_inc(loads_begun, 1)
                        load_v(h + 1, p)
                for p in range(NP):
                    store(HEADS - 1, p)
                sp.wait_ge(S["md"], HEADS + START)
                for p in range(NP):
                    views = by_token(D["md"][p].rearrange("s h c -> s (h c)"), p)
                    for r, view in enumerate(views):
                        n = TILES // len(views)
                        sp.dma_start(view, md_all[:, p, r * n:(r + 1) * n].rearrange("p t h c -> p t (h c)")
                                     ).then_inc(md_stored, 16)
                for p in range(NP):
                    sp.wait_ge(stored[p], STORES[p] * (HEADS + 1))
                sp.wait_ge(md_stored, sum(STORES))

            @block.scalar
            def _(act):
                def prepare(h):
                    for g in range(8):
                        act.wait_ge(S["prep_turn"], h * 8 + (g + 1 + START))
                        cols = slice(g % 4 * 512, g % 4 * 512 + 512)
                        out = kt[:, 0, EDGE + cols.start:EDGE + cols.stop] if g < 4 else qs[:, cols]
                        nc.scalar.copy(out, scores[:, g % 4].rearrange("p s k -> p (s k)")).then_inc(S["prep_hi"], 1)

                def exp(n, w):
                    act.wait_ge(S["negmax"], n + (w + 1 + START))
                    act.wait_ge(S["e_turn"], n + (w - 3 + START))
                    p = pattern(w)
                    for s in range(2):
                        t = w % PAIRS * 2 + s
                        nc.scalar.activation(used(w, e[:, w % 4])[:, s], used(w, masked[:, w % 4])[:, s], ACT.Exp,
                                             bias=neg_max[:, w % 4, s:s + 1], scale=SCALE,
                                             accum_out=md_head[:, p, t, 1:2]).then_inc(S["exp"], 1)

                def e_hi(n, w):
                    act.wait_ge(S["e_turn"], n + (w + 1 + START))
                    act.wait_ge(S["pv"], n + (w - 1 + START))
                    c = 4 if pattern(w) < 2 else 2
                    nc.scalar.copy(et_hi[:, w % 2, :c], turned[:, w % 2, :c]).then_inc(S["e_hi"], 1)

                def step(h, n, w):
                    if w == 0:
                        act.wait_ge(S["md"], h + START)
                    if w < WORK:
                        exp(n, w)
                    if 2 <= w < WORK + 2:
                        e_hi(n, w - 2)

                for name in "prep_hi exp e_hi".split():
                    act.sem_inc(S[name], START)
                heads(act, prepare, step)

            @block.vector
            def _(dve):
                def prepare(h):
                    for g in range(8):
                        dve.wait_ge(S["prep_hi"], h * 8 + (g + 1 + START))
                        cols = slice(g % 4 * 512, g % 4 * 512 + 512)
                        src = scores[:, g % 4].rearrange("p s k -> p (s k)")
                        if g < 4:
                            edge = slice(EDGE + cols.start, EDGE + cols.stop)
                            nc.vector.tensor_tensor(kt[:, 1, edge], src, kt[:, 0, edge].bitcast(F32),
                                                    ALU.subtract).then_inc(S["prep_lo"], 1)
                        else:
                            nc.vector.tensor_tensor(qs[HD:, cols], src[HD:], qs[HD:, cols].bitcast(F32),
                                                    ALU.subtract).then_inc(S["prep_lo"], 1)
                    dve.wait_ge(S["md"], h + START)

                def mask(n, w):
                    dve.wait_ge(S["scored"], n + (w + 1 + START))
                    dve.wait_ge(S["exp"], n * 2 + (2 * w - 6 + START))
                    dve.sem_inc(masks_begun, 1)
                    p = pattern(w)
                    for s in range(2):
                        j, t = tile_of(w, s)[1], w % PAIRS * 2 + s
                        if SUB[p] == 1:
                            allowed, found = masks[:, 3, RADIUS:RADIUS + P], scores[:, w % 4, s, s * P:s * P + P]
                        else:
                            allowed = masks[:, 0 if j == 0 else 2 if j == SUB[p] - 1 else 1]
                            found = scores[:, w % 4, s]
                        nc.vector.tensor_tensor_reduce(used(w, masked[:, w % 4])[:, s], found, allowed, 1.0, -3e38,
                                                       ALU.add, ALU.max, md_head[:, p, t, 0:1]).then_inc(S["masked"], 1)
                    dve.wait_ge(S["masked"], n * 2 + (2 * w + 2 + START))
                    t = w % PAIRS * 2
                    nc.vector.tensor_scalar(neg_max[:, w % 4], md_head[:, p, t:t + 2, 0], -SCALE, None,
                                            ALU.mult).then_inc(S["negmax"], 1)

                def e_lo(n, w):
                    dve.wait_ge(S["e_hi"], n + (w + 1 + START))
                    c = 4 if pattern(w) < 2 else 2
                    nc.vector.tensor_tensor(et_lo[:, w % 2, :c], turned[:, w % 2, :c], et_hi[:, w % 2, :c].bitcast(F32),
                                            ALU.subtract).then_inc(S["e_lo"], 1)

                def output(h, n, w):
                    p = pattern(w)
                    dve.wait_ge(S["pv"], n + (w + 1 + START))
                    if w % PAIRS == 0:
                        dve.wait_ge(stored[p], h * STORES[p] + STORES[p])
                    t = w % PAIRS * 2
                    nc.vector.tensor_reduce(nout[:, p, t:t + 2], pv[:, w % 2, :, :2 * HD].rearrange(
                        "p s (u d) -> p s d u", u=2), AX.X, ALU.add).then_inc(S["out"], 1)

                def step(h, n, w):
                    if w < WORK:
                        mask(n, w)
                    if 2 <= w < WORK + 2:
                        e_lo(n, w - 2)
                    if w >= 3:
                        output(h, n, w - 3)
                    if w == WORK + 2:
                        dve.wait_ge(S["exp"], n * 2 + (2 * WORK + START))
                        nc.vector.tensor_copy(md_all[:, :, :, bass.ts(h, 1)].rearrange("p k t h c -> p (k t) (h c)"),
                                              md_head[:].rearrange("p k t c -> p (k t) c")).then_inc(S["md"], 1)

                for name in "prep_lo masked negmax e_lo out md".split():
                    dve.sem_inc(S[name], START)
                dve.wait_ge(const_in, 32)
                heads(dve, prepare, step)

            @block.gpsimd
            def _(pool):
                def zero(k, t):
                    if k:
                        pool.wait_ge(zeroed, k)
                    nc.gpsimd.memset(t.bitcast(F32), 0.0).then_inc(zeroed, 1)

                zero(0, kt[:, :, :EDGE])
                zero(1, kt[:, :, EDGE + SEQ:])
                for p in range(2):
                    d, b = PATTERNS[p][1], BASE[p]
                    v = v_hl[:, b:b + CHUNKS[p] * d].rearrange("p (r c) x -> p r c x", r=d)
                    zero(2 + 2 * p, v[:RADIUS, :, 0])
                    zero(3 + 2 * p, v[RADIUS:, :, SUB[p]])

            @block.tensor
            def _(pe):
                def prepare(h):
                    pe.wait_ge(raw_in, h * 32 + 32)
                    for g in range(8):
                        if g < 4:
                            pe.wait_ge(S["masked"], h * (WORK * 2) + START)
                        else:
                            pe.wait_ge(S["prep_lo"], h * 8 + (g - 3 + START))
                        for c in range(4):
                            ins = nc.tensor.transpose(scores[:, g % 4, c // 2, c % 2 * P:c % 2 * P + P],
                                                      raw[:, g // 4, g % 4 * 4 + c], ident[:])
                        ins.then_inc(S["prep_turn"], 1)
                    pe.wait_ge(S["prep_lo"], h * 8 + (8 + START))

                def score(n, w):
                    if w >= 4:
                        pe.wait_ge(S["masked"], n * 2 + (2 * w - 6 + START))
                    p = pattern(w)
                    d = PATTERNS[p][1]
                    for s in range(2):
                        r, j = tile_of(w, s)
                        first = j * P * d + r
                        queries = qs[:, first:first + (P - 1) * d + 1:d]
                        out = scores[:, w % 4, s]
                        for u in range(2):
                            if SUB[p] == 1:
                                r0 = r - s
                                keys = kt[:, u, EDGE:EDGE + SEQ].rearrange("p (k r) -> p r k", r=d)[:, r0:r0 + 2]
                                dst = out.rearrange("p (r k) -> p r k", r=2)
                            else:
                                start = EDGE + first - RADIUS * d
                                keys, dst = kt[:, u, start:start + (KEYS - 1) * d + 1:d], out
                            ins = nc.tensor.matmul(dst, queries, keys, start=(u == 0), stop=(u == 1))
                    ins.then_inc(S["scored"], 1)

                def turn(n, w):
                    pe.wait_ge(S["exp"], n * 2 + (2 * w + 2 + START))
                    pe.wait_ge(S["e_lo"], n + (w - 1 + START))
                    for s in range(2):
                        chunks = 2 if pattern(w) < 2 else 1
                        for c in range(chunks):
                            ins = nc.tensor.transpose(turned[:, w % 2, s * chunks + c],
                                                      e[:, w % 4, s, c * P:(c + 1) * P], ident[:])
                    ins.then_inc(S["e_turn"], 1)

                def values(h, n, w):
                    p = pattern(w)
                    if w % PAIRS == 0:
                        pe.wait_ge(v_in[p], h * V_LOADS[p] + V_LOADS[p])
                    pe.wait_ge(S["e_lo"], n + (w + 1 + START))
                    pe.wait_ge(S["out"], n + (w - 1 + START))
                    chunks = 2 if p < 2 else 1
                    for s in range(2):
                        r, j = tile_of(w, s)
                        for c in range(chunks):
                            v = v_hl[:, BASE[p] + r * CHUNKS[p] + j + c].unsqueeze(1).to_broadcast([P, 2, 2 * HD])
                            dst = pv[:, w % 2, s].rearrange("p (u x) -> p u x", u=2)
                            nc.tensor.matmul(dst, et_hi[:, w % 2, s * chunks + c], v, start=(c == 0), stop=False)
                            ins = nc.tensor.matmul(dst, et_lo[:, w % 2, s * chunks + c], v,
                                                   start=False, stop=(c == chunks - 1))
                    ins.then_inc(S["pv"], 1)

                def step(h, n, w):
                    if w < WORK:
                        score(n, w)
                    if 2 <= w < WORK + 2:
                        turn(n, w - 2)
                    if w >= 3:
                        values(h, n, w - 3)

                for name in "prep_turn scored e_turn pv".split():
                    pe.sem_inc(S[name], START)
                pe.wait_ge(const_in, 32)
                pe.wait_ge(zeroed, 6)
                heads(pe, prepare, step)


def one_pass(eng, pair):
    with eng.Fori(0, PAIRS - 1) as i:
        pair(i, False)
    pair(PAIRS - 1, True)


def lagged_pass(eng, step, end):
    step(Tile(0, 0, 0), True, 2)
    with eng.Fori(0, PAIRS - 2) as i:
        step(Tile(i, i, 1), False, 2)
        step(Tile(i + 1, i + 1, 0), False, 2)
    for t in range(TILES - 3, TILES):
        step(Tile(t // 2, t // 2, t % 2), False, min(2, TILES - 1 - t))
    end(Tile(PAIRS - 1, PAIRS - 1, 1))


def mix_phase(kit):
    nc, D = kit.nc, kit.dram
    G, NP, H = 2, len(PATTERNS), MAPS
    with ExitStack() as mem:
        sb = lambda name, shape, dt=F32: mem.enter_context(nc.sbuf_tensor("d_" + name, shape, dt))
        ps = lambda name, shape: mem.enter_context(nc.psum_tensor("d_" + name, shape, F32))
        w_raw = sb("w_raw", [P, KC, GROUP])
        w_hi = sb("w_hi", [P, G, KC, GROUP], F32R)
        w_lo = sb("w_lo", [P, G, KC, GROUP], F32R)
        ident = sb("ident", [P, P])
        gain = sb("gain", [P, DM])
        half = sb("half", [P, 1])
        x = sb("x", [P, 2, DM])
        mixed = sb("mixed", [P, 2, DM])
        nd = sb("nd", [P, 2, NP * H, HD])
        md = sb("md", [P, 2, NP, H, 2])
        top = sb("top", [P, H])
        below = sb("below", [P, NP, H])
        weight = sb("weight", [P, NP, H])
        wden = sb("wden", [P, NP, H])
        total = sb("total", [P, H])
        rtotal = sb("rtotal", [P, H])
        share = sb("share", [P, NP, H])
        parts = sb("parts", [P, NP, H * HD])
        two = sb("two", [P, H * HD])
        mt_hi = sb("mt_hi", [P, 2, KC, P], F32R)
        mt_lo = sb("mt_lo", [P, 2, KC, P], F32R)
        h = sb("h", [P, 2, DM])
        junk = sb("junk", [P, DM])
        ssq, mean, rstd = (sb(s, [P, 2]) for s in ("ssq", "mean", "rstd"))
        hn = sb("hn", [P, 2, DM])
        xt_hi = sb("xt_hi", [P, 2, KC, P], F32R)
        xt_lo = sb("xt_lo", [P, 2, KC, P], F32R)
        m_turned = ps("m_turned", [P, 2, 4 * P])
        h_turned = ps("h_turned", [P, 2, 4 * P])
        acc = ps("acc", [P, 2, G, GROUP])

        const_in, w_in, half_set = kit.sem("d_const_in"), kit.sem("d_w_in"), kit.sem("d_half_set")
        x_in, nd_in, h_stored, xt_stored = (kit.sem_pair("d_" + s) for s in ("x_in", "nd_in", "h_stored", "xt_stored"))
        od_in = kit.sem_pair("d_od_in")
        names = ("w_hi w_lo top below weight wden total rtotal share parts two merged m_turn m_hi m_lo acc h ssq "
                 "mean rstd hn h_turn h_hi h_lo")
        S = {name: kit.sem("d_" + name) for name in names.split()}

        with nc.Block() as block:

            @block.sync
            def _(sp):
                def load(a):
                    sp.wait_ge(S["h"], a.n * 2 - 2 + START)
                    sp.dma_start(x[:, a.s], D["x"][bass.ts(a.t, P)]).then_inc(x_in[a.s], 16)

                def load_attention(a):
                    sp.wait_ge(S["parts"], a.n - 1 + START)
                    sp.wait_ge(S["m_turn"], a.n * 2 - 2 + START)
                    for k in range(NP):
                        sp.dma_start(nd[:, a.s, k * H:(k + 1) * H], D["nd"][k, bass.ts(a.t, P)]).then_inc(nd_in[a.s], 16)
                    sp.dma_start(md[:, a.s].rearrange("p k h c -> p k (h c)"), D["md"][:, bass.ts(a.t, P)].rearrange(
                        "k p h c -> p k (h c)")).then_inc(nd_in[a.s], 16)
                    sp.dma_start(mixed[:, a.s, :GROUP], D["od"][bass.ts(a.t, P)]).then_inc(od_in[a.s], 16)

                def store(a):
                    sp.wait_ge(S["h"], a.n * 2 + (2 + START))
                    sp.dma_start(D["h"][bass.ts(a.t, P)], h[:, a.s]).then_inc(h_stored[a.s], 16)

                def store_turned(a):
                    sp.wait_ge(S["h_lo"], a.n * 2 + (2 + START))
                    sp.dma_start(D["xt_hi"][a.t], xt_hi[:, a.s].bitcast(F32)).then_inc(xt_stored[a.s], 16)
                    sp.dma_start(D["xt_lo"][a.t], xt_lo[:, a.s].bitcast(F32)).then_inc(xt_stored[a.s], 16)

                for s in range(2):
                    sp.sem_inc(h_stored[s], 16)
                    sp.sem_inc(xt_stored[s], 32)
                load_attention(Tile(0, 0, 0))
                sp.dma_start(ident[:], D["ident"][:]).then_inc(const_in, 16)
                sp.dma_start(gain[:], D["g_mlp"].partition_broadcast(P)).then_inc(const_in, 16)
                for g in range(G):
                    sp.wait_ge(S["w_lo"], g + START)
                    sp.dma_start(w_raw[:], D["w_out"][:, g * GROUP:(g + 1) * GROUP].rearrange(
                        "(c p) n -> p c n", p=P)).then_inc(w_in, 16)
                    if g == 0:
                        load_attention(Tile(0, 0, 1))
                        load(Tile(0, 0, 0))
                        load(Tile(0, 0, 1))

                def step(a, first, more):
                    if more == 2:
                        load_attention(a.next(2))
                    store(a)
                    if more == 2:
                        load(a.next(2))
                    if not first:
                        store_turned(a.before())

                lagged_pass(sp, step, store_turned)
                for s in range(2):
                    sp.wait_ge(h_stored[s], 16 * (PAIRS + 1))
                    sp.wait_ge(xt_stored[s], 32 * (PAIRS + 1))

            @block.scalar
            def _(act):
                def split_w(g):
                    act.wait_ge(w_in, 16 * (g + 1))
                    nc.scalar.copy(w_hi[:, g], w_raw[:]).then_inc(S["w_hi"], 1)

                def weigh(a):
                    act.wait_ge(S["below"], a.n + (1 + START))
                    act.wait_ge(S["share"], a.n + START)
                    nc.scalar.activation(weight[:], below[:], ACT.Exp, scale=SCALE).then_inc(S["weight"], 1)

                def m_hi(a):
                    act.wait_ge(S["acc"], a.n * 2 - 2 + START)
                    for b in range(2):
                        act.wait_ge(S["m_turn"], a.n * 2 + (b + 1 + START))
                        nc.scalar.copy(mt_hi[:, a.s, 4 * b:4 * b + 4].rearrange("p c t -> p (c t)"),
                                       m_turned[:, b]).then_inc(S["m_hi"], 1)

                def square(a):
                    act.wait_ge(S["h"], a.n * 2 + (2 + START))
                    act.wait_ge(S["ssq"], a.n + START)
                    nc.scalar.activation(junk[:], h[:, a.s], ACT.Square,
                                         accum_out=ssq[:, a.s:a.s + 1]).then_inc(S["ssq"], 1)

                def h_hi(a):
                    act.wait_ge(xt_stored[a.s], a.j * 32 + 32)
                    for b in range(2):
                        act.wait_ge(S["h_turn"], a.n * 2 + (b + 1 + START))
                        nc.scalar.copy(xt_hi[:, a.s, 4 * b:4 * b + 4].rearrange("p c t -> p (c t)"),
                                       h_turned[:, b]).then_inc(S["h_hi"], 1)

                for name in "w_hi weight m_hi ssq h_hi".split():
                    act.sem_inc(S[name], START)
                weigh(Tile(0, 0, 0))
                split_w(0)
                m_hi(Tile(0, 0, 0))
                split_w(1)
                weigh(Tile(0, 0, 1))

                def step(a, first, more):
                    if more:
                        m_hi(a.next(1))
                    if more == 2:
                        weigh(a.next(2))
                    square(a)
                    if not first:
                        h_hi(a.before())

                lagged_pass(act, step, h_hi)

            @block.vector
            def _(dve):
                def split_w(g):
                    dve.wait_ge(S["w_hi"], g + 1 + START)
                    nc.vector.tensor_tensor(w_lo[:, g], w_raw[:], w_hi[:, g].bitcast(F32),
                                            ALU.subtract).then_inc(S["w_lo"], 1)

                def maxima(a):
                    dve.wait_ge(nd_in[a.s], a.j * 64 + 64)
                    dve.wait_ge(S["below"], a.n + START)
                    nc.vector.tensor_reduce(top[:], md[:, a.s, :, :, 0].rearrange("p k h -> p h k"),
                                            AX.X, ALU.max).then_inc(S["top"], 1)
                    dve.wait_ge(S["top"], a.n + (1 + START))
                    dve.wait_ge(S["weight"], a.n + START)
                    nc.vector.tensor_tensor(below[:], md[:, a.s, :, :, 0], top[:].unsqueeze(1).to_broadcast([P, NP, H]),
                                            ALU.subtract).then_inc(S["below"], 1)

                def merge(a):
                    dve.wait_ge(S["weight"], a.n + (1 + START))
                    nc.vector.tensor_tensor(wden[:], weight[:], md[:, a.s, :, :, 1], ALU.mult).then_inc(S["wden"], 1)
                    dve.wait_ge(S["wden"], a.n + (1 + START))
                    nc.vector.tensor_reduce(total[:], wden[:].rearrange("p k h -> p h k"),
                                            AX.X, ALU.add).then_inc(S["total"], 1)
                    dve.wait_ge(S["total"], a.n + (1 + START))
                    nc.vector.reciprocal(rtotal[:], total[:]).then_inc(S["rtotal"], 1)
                    dve.wait_ge(S["rtotal"], a.n + (1 + START))
                    nc.vector.tensor_tensor(share[:], weight[:], rtotal[:].unsqueeze(1).to_broadcast([P, NP, H]),
                                            ALU.mult).then_inc(S["share"], 1)
                    dve.wait_ge(S["share"], a.n + (1 + START))
                    dve.wait_ge(S["merged"], a.n + START)
                    nc.vector.tensor_tensor(
                        parts[:].rearrange("p k (h d) -> p (k h) d", d=HD), nd[:, a.s],
                        share[:].rearrange("p k h -> p (k h)").unsqueeze(2).to_broadcast([P, NP * H, HD]),
                        ALU.mult).then_inc(S["parts"], 1)

                def lo(a, bank, hi, out, done_hi, done):
                    for b in range(2):
                        dve.wait_ge(S[done_hi], a.n * 2 + (b + 1 + START))
                        view = lambda t: t[:, a.s, 4 * b:4 * b + 4].rearrange("p c t -> p (c t)")
                        nc.vector.tensor_tensor(view(out), bank[:, b], view(hi).bitcast(F32),
                                                ALU.subtract).then_inc(S[done], 1)

                def residual(a):
                    dve.wait_ge(x_in[a.s], a.j * 16 + 16)
                    dve.wait_ge(h_stored[a.s], a.j * 16 + 16)
                    for g in range(G):
                        dve.wait_ge(S["acc"], a.n * 2 + (g + 1 + START))
                        cols = slice(g * GROUP, (g + 1) * GROUP)
                        nc.vector.tensor_tensor(h[:, a.s, cols], acc[:, a.s, g], x[:, a.s, cols],
                                                ALU.add).then_inc(S["h"], 1)

                def normalise(a):
                    v = slice(a.s, a.s + 1)
                    dve.wait_ge(S["ssq"], a.n + (1 + START))
                    nc.vector.tensor_scalar(mean[:, v], ssq[:, v], 1.0 / DM, NORM_EPS,
                                            ALU.mult, ALU.add).then_inc(S["mean"], 1)
                    dve.wait_ge(S["rstd"], a.n + (1 + START))
                    dve.wait_ge(S["h_turn"], a.n * 2 - 2 + START)
                    nc.vector.scalar_tensor_tensor(out=hn[:, a.s], in0=h[:, a.s], scalar=rstd[:, v], in1=gain[:],
                                                   op0=ALU.mult, op1=ALU.mult).then_inc(S["hn"], 1)

                for name in "w_lo top below wden total rtotal share parts m_lo h mean hn h_lo".split():
                    dve.sem_inc(S[name], START)
                dve.wait_ge(const_in, 32)
                maxima(Tile(0, 0, 0))
                merge(Tile(0, 0, 0))
                split_w(0)
                lo(Tile(0, 0, 0), m_turned, mt_hi, mt_lo, "m_hi", "m_lo")
                split_w(1)
                maxima(Tile(0, 0, 1))
                merge(Tile(0, 0, 1))

                def step(a, first, more):
                    if more:
                        lo(a.next(1), m_turned, mt_hi, mt_lo, "m_hi", "m_lo")
                    if more == 2:
                        maxima(a.next(2))
                        merge(a.next(2))
                    residual(a)
                    normalise(a)
                    if not first:
                        lo(a.before(), h_turned, xt_hi, xt_lo, "h_hi", "h_lo")

                lagged_pass(dve, step, lambda a: lo(a, h_turned, xt_hi, xt_lo, "h_hi", "h_lo"))

            @block.gpsimd
            def _(pool):
                def merge(a):
                    pool.wait_ge(S["parts"], a.n + (1 + START))
                    nc.gpsimd.tensor_tensor(two[:], parts[:, 0], parts[:, 1], ALU.add).then_inc(S["two"], 1)
                    pool.wait_ge(S["two"], a.n + (1 + START))
                    pool.wait_ge(S["m_turn"], a.n * 2 - 2 + START)
                    nc.gpsimd.tensor_tensor(mixed[:, a.s, GROUP:], two[:], parts[:, 2], ALU.add).then_inc(S["merged"], 1)

                def root(a):
                    v = slice(a.s, a.s + 1)
                    pool.wait_ge(S["mean"], a.n + (1 + START))
                    nc.gpsimd.tensor_tensor(rstd[:, v], mean[:, v], half[:], ALU.pow).then_inc(S["rstd"], 1)

                for name in "two merged rstd".split():
                    pool.sem_inc(S[name], START)
                nc.gpsimd.memset(half[:], -0.5).then_inc(half_set, 1)
                pool.wait_ge(half_set, 1)
                merge(Tile(0, 0, 0))
                merge(Tile(0, 0, 1))

                def step(a, first, more):
                    if more == 2:
                        merge(a.next(2))
                    root(a)

                lagged_pass(pool, step, lambda a: None)

            @block.tensor
            def _(pe):
                def turn(a, bank, src, before, done, gate):
                    gate(a)
                    for b in range(2):
                        pe.wait_ge(S[before], a.n * 2 + (b - 1 + START))
                        for c in range(4):
                            ins = nc.tensor.transpose(bank[:, b, c * P:(c + 1) * P],
                                                      src[:, a.s, (4 * b + c) * P:(4 * b + c + 1) * P], ident[:])
                        ins.then_inc(S[done], 1)

                def mixed_ready(a):
                    pe.wait_ge(S["merged"], a.n + (1 + START))
                    pe.wait_ge(od_in[a.s], a.j * 16 + 16)

                def hn_ready(a):
                    pe.wait_ge(S["hn"], a.n + (1 + START))

                def project(a):
                    pe.wait_ge(S["m_lo"], a.n * 2 + (2 + START))
                    for g in range(G):
                        pe.wait_ge(S["w_lo"], g + 1 + START)
                        pe.wait_ge(S["h"], a.n * 2 + (g - 3 + START))
                        for c in range(KC):
                            ins = matmul3(nc, acc[:, a.s, g], mt_hi[:, a.s, c], mt_lo[:, a.s, c],
                                          w_hi[:, g, c], w_lo[:, g, c], c == 0, c == KC - 1)
                        ins.then_inc(S["acc"], 1)

                for name in "m_turn acc h_turn".split():
                    pe.sem_inc(S[name], START)
                pe.wait_ge(const_in, 32)
                turn(Tile(0, 0, 0), m_turned, mixed, "m_lo", "m_turn", mixed_ready)

                def turn_h(a):
                    turn(a, h_turned, hn, "h_lo", "h_turn", hn_ready)

                def step(a, first, more):
                    if more:
                        turn(a.next(1), m_turned, mixed, "m_lo", "m_turn", mixed_ready)
                    project(a)
                    if not first:
                        turn_h(a.before())

                lagged_pass(pe, step, turn_h)


def mlp_phase(kit):
    nc, D = kit.nc, kit.dram
    FB, FT, TB = D_FF // 256, 2, 2
    HALVES, HT = 2, TILES // 2
    with ExitStack() as mem:
        sb = lambda name, shape, dt=F32: mem.enter_context(nc.sbuf_tensor("e_" + name, shape, dt))
        ps = lambda name, shape: mem.enter_context(nc.psum_tensor("e_" + name, shape, F32))
        xt_hi = sb("xt_hi", [P, KC, HT * P], F32R)
        xt_lo = sb("xt_lo", [P, KC, HT * P], F32R)
        h = sb("h", [P, HT, DM])
        up_raw = sb("up_raw", [P, KC, 256])
        up_hi, up_lo = sb("up_hi", [P, KC, 256], F32R), sb("up_lo", [P, KC, 256], F32R)
        down_raw = sb("down_raw", [P, FT, DM])
        down_hi, down_lo = sb("down_hi", [P, FT, DM], F32R), sb("down_lo", [P, FT, DM], F32R)
        r = sb("r", [P, 2, 512])
        sq = sb("sq", [P, 2, 512])
        u_hi = sb("u_hi", [P, FT, HT * P], F32R)
        u_lo = sb("u_lo", [P, FT, HT * P], F32R)
        up_acc = ps("up_acc", [P, 2, 512])
        down_acc = ps("down_acc", [P, 4, 512])

        xt_in, h_in, stored = kit.sem("e_xt_in"), kit.sem("e_h_in"), kit.sem("e_stored")
        up_in, down_in = kit.sem("e_up_in"), kit.sem("e_down_in")
        names = "up_hi up_lo down_hi down_lo up_acc relu sq u_hi u_lo down_acc h"
        S = {name: kit.sem("e_" + name) for name in names.split()}
        UNITS = [(f, t) for t in range(TB) for f in range(FT)]
        DU = HT * 2

        def blocks(eng, start, block_step, end):
            with eng.Fori(0, HALVES) as z:
                start(z)
                with eng.Fori(0, FB) as f:
                    block_step(z, f, z * FB + f)
                end(z)

        with nc.Block() as block:

            @block.sync
            def _(sp):
                def start(z):
                    sp.wait_ge(S["up_acc"], z * (FB * 4) + START)
                    for k in range(HT):
                        for src, dst in ((D["xt_hi"], xt_hi[:].bitcast(F32)), (D["xt_lo"], xt_lo[:].bitcast(F32))):
                            sp.dma_start(dst[:, :, k * P:(k + 1) * P], src[z * HT + k]).then_inc(xt_in, 16)
                    sp.wait_ge(stored, z * 16 + 16)
                    sp.dma_start(h[:], D["h"].rearrange("(z t p) d -> z p t d", z=HALVES, p=P)[z]).then_inc(h_in, 16)

                def step(z, f, n):
                    sp.wait_ge(S["up_lo"], n + START)
                    sp.dma_start(up_raw[:], D["w_up"].rearrange("(c p) (f n) -> f p c n", p=P, n=256)[f]
                                 ).then_inc(up_in, 16)
                    sp.wait_ge(S["down_lo"], n + START)
                    sp.dma_start(down_raw[:], D["w_down"].rearrange("(f c p) d -> f p c d", p=P, c=FT)[f]
                                 ).then_inc(down_in, 16)

                def end(z):
                    sp.wait_ge(S["h"], z * (FB * DU) + (FB * DU + START))
                    sp.dma_start(D["h2"].rearrange("(z t p) d -> z p t d", z=HALVES, p=P)[z], h[:]).then_inc(stored, 16)

                sp.sem_inc(stored, 16)
                blocks(sp, start, step, end)
                sp.wait_ge(stored, 16 * (HALVES + 1))

            @block.scalar
            def _(act):
                def step(z, f, n):
                    act.wait_ge(up_in, n * 16 + 16)
                    act.wait_ge(S["up_acc"], n * 4 + START)
                    nc.scalar.copy(up_hi[:], up_raw[:]).then_inc(S["up_hi"], 1)
                    act.wait_ge(down_in, n * 16 + 16)
                    act.wait_ge(S["down_acc"], n * DU + START)
                    nc.scalar.copy(down_hi[:], down_raw[:]).then_inc(S["down_hi"], 1)
                    for k, (ft, tb) in enumerate(UNITS):
                        act.wait_ge(S["up_acc"], n * 4 + (k + 1 + START))
                        act.wait_ge(S["sq"], n * 4 + (k - 1 + START))
                        nc.scalar.activation(r[:, k % 2], up_acc[:, k % 2], ACT.Relu).then_inc(S["relu"], 1)
                        act.wait_ge(S["sq"], n * 4 + (k + 1 + START))
                        nc.scalar.copy(u_hi[:, ft, tb * 512:(tb + 1) * 512], sq[:, k % 2]).then_inc(S["u_hi"], 1)

                for name in "up_hi down_hi relu u_hi".split():
                    act.sem_inc(S[name], START)
                blocks(act, lambda z: None, step, lambda z: None)

            @block.vector
            def _(dve):
                def step(z, f, n):
                    dve.wait_ge(S["up_hi"], n + (1 + START))
                    nc.vector.tensor_tensor(up_lo[:], up_raw[:], up_hi[:].bitcast(F32),
                                            ALU.subtract).then_inc(S["up_lo"], 1)
                    dve.wait_ge(S["down_hi"], n + (1 + START))
                    nc.vector.tensor_tensor(down_lo[:], down_raw[:], down_hi[:].bitcast(F32),
                                            ALU.subtract).then_inc(S["down_lo"], 1)
                    for k in range(DU):
                        t, g = k // 2, k % 2
                        dve.wait_ge(S["down_acc"], n * DU + (k + 1 + START))
                        if k == 0:
                            dve.wait_ge(h_in, z * 16 + 16)
                            dve.wait_ge(S["h"], n * DU + START)
                        cols = slice(g * 512, (g + 1) * 512)
                        nc.vector.tensor_tensor(h[:, t, cols], down_acc[:, k % 4], h[:, t, cols],
                                                ALU.add).then_inc(S["h"], 1)

                for name in "up_lo down_lo h".split():
                    dve.sem_inc(S[name], START)
                blocks(dve, lambda z: None, step, lambda z: None)

            @block.gpsimd
            def _(pool):
                def step(z, f, n):
                    for k, (ft, tb) in enumerate(UNITS):
                        pool.wait_ge(S["relu"], n * 4 + (k + 1 + START))
                        pool.wait_ge(S["u_lo"], n * 4 + (k - 1 + START))
                        nc.gpsimd.tensor_tensor(sq[:, k % 2], r[:, k % 2], r[:, k % 2], ALU.mult).then_inc(S["sq"], 1)
                        pool.wait_ge(S["u_hi"], n * 4 + (k + 1 + START))
                        cols = slice(tb * 512, (tb + 1) * 512)
                        nc.gpsimd.tensor_tensor(u_lo[:, ft, cols], sq[:, k % 2], u_hi[:, ft, cols].bitcast(F32),
                                                ALU.subtract).then_inc(S["u_lo"], 1)

                for name in "sq u_lo".split():
                    pool.sem_inc(S[name], START)
                blocks(pool, lambda z: None, step, lambda z: None)

            @block.tensor
            def _(pe):
                def step(z, f, n):
                    pe.wait_ge(xt_in, z * (HT * 32) + HT * 32)
                    pe.wait_ge(S["up_lo"], n + (1 + START))
                    for k, (ft, tb) in enumerate(UNITS):
                        pe.wait_ge(S["relu"], n * 4 + (k - 1 + START))
                        cols = slice(tb * 512, (tb + 1) * 512)
                        for c in range(KC):
                            ins = matmul3(nc, up_acc[:, k % 2], up_hi[:, c, ft * P:(ft + 1) * P],
                                          up_lo[:, c, ft * P:(ft + 1) * P], xt_hi[:, c, cols], xt_lo[:, c, cols],
                                          c == 0, c == KC - 1)
                        ins.then_inc(S["up_acc"], 1)
                    pe.wait_ge(S["down_lo"], n + (1 + START))
                    for k in range(DU):
                        t, g = k // 2, k % 2
                        if k % (DU // TB) == 0:
                            pe.wait_ge(S["u_lo"], n * 4 + ((k // (DU // TB) + 1) * FT + START))
                        pe.wait_ge(S["h"], n * DU + (k - 3 + START))
                        toks, cols = slice(t * P, (t + 1) * P), slice(g * 512, (g + 1) * 512)
                        for c in range(FT):
                            ins = matmul3(nc, down_acc[:, k % 4], u_hi[:, c, toks], u_lo[:, c, toks],
                                          down_hi[:, c, cols], down_lo[:, c, cols], c == 0, c == FT - 1)
                        ins.then_inc(S["down_acc"], 1)

                for name in "up_acc down_acc".split():
                    pe.sem_inc(S[name], START)
                blocks(pe, lambda z: None, step, lambda z: None)


def gate_phase(kit):
    nc, D = kit.nc, kit.dram
    G, PC = 2, D_PLE // P
    with ExitStack() as mem:
        sb = lambda name, shape, dt=F32: mem.enter_context(nc.sbuf_tensor("f_" + name, shape, dt))
        ps = lambda name, shape: mem.enter_context(nc.psum_tensor("f_" + name, shape, F32))
        w_raw = sb("w_raw", [P, KC, GROUP])
        w_hi, w_lo = sb("w_hi", [P, G, KC, GROUP], F32R), sb("w_lo", [P, G, KC, GROUP], F32R)
        e_raw = sb("e_raw", [P, PC, DM])
        e_hi, e_lo = sb("e_hi", [P, PC, DM], F32R), sb("e_lo", [P, PC, DM], F32R)
        ident = sb("ident", [P, P])
        gain, gain_final = sb("gain", [P, DM]), sb("gain_final", [P, DM])
        half = sb("half", [P, 1])
        h, hn = sb("h", [P, 2, DM]), sb("hn", [P, 2, DM])
        res = sb("res", [P, 2, DM])
        emb = sb("emb", [P, 2, D_PLE])
        junk, junk2 = sb("junk", [P, DM]), sb("junk2", [P, DM])
        ssq, mean, rstd = (sb(s, [P, 2]) for s in ("ssq", "mean", "rstd"))
        ssq2, mean2, rstd2 = (sb(s, [P, 2]) for s in ("ssq2", "mean2", "rstd2"))
        xt_hi, xt_lo = sb("xt_hi", [P, 2, KC, P], F32R), sb("xt_lo", [P, 2, KC, P], F32R)
        et_hi, et_lo = sb("et_hi", [P, 2, PC, P], F32R), sb("et_lo", [P, 2, PC, P], F32R)
        gate = sb("gate", [P, G, GROUP])
        gated = sb("gated", [P, G, GROUP])
        h3 = sb("h3", [P, 2, DM])
        out = sb("out", [P, 2, DM])
        turned = ps("turned", [P, 2, 4 * P])
        e_turned = ps("e_turned", [P, 4 * P])
        gate_acc, emb_acc = ps("gate_acc", [P, G, GROUP]), ps("emb_acc", [P, G, GROUP])

        const_in, w_in, e_in, half_set = (kit.sem("f_" + s) for s in ("const_in", "w_in", "e_in", "half_set"))
        h_in, res_in, emb_in, stored = (kit.sem_pair("f_" + s) for s in ("h_in", "res_in", "emb_in", "stored"))
        names = ("w_hi w_lo e_whi e_wlo ssq mean rstd hn turn hi lo e_turn e_hi e_lo gate_acc emb_acc gate gated h3 "
                 "ssq2 mean2 rstd2 out")
        S = {name: kit.sem("f_" + name) for name in names.split()}

        with nc.Block() as block:

            @block.sync
            def _(sp):
                def load(a):
                    sp.wait_ge(S["hn"], a.n - 1 + START)
                    sp.dma_start(h[:, a.s], D["h2"][bass.ts(a.t, P)]).then_inc(h_in[a.s], 16)
                    sp.wait_ge(S["e_turn"], a.n - 1 + START)
                    sp.dma_start(emb[:, a.s], D["p"][bass.ts(a.t, P)]).then_inc(emb_in[a.s], 16)

                def load_again(a):
                    sp.wait_ge(S["h3"], a.n * 2 - 2 + START)
                    sp.dma_start(res[:, a.s], D["h2"][bass.ts(a.t, P)]).then_inc(res_in[a.s], 16)

                def store(a):
                    sp.wait_ge(S["out"], a.n + (1 + START))
                    sp.dma_start(D["out"][bass.ts(a.t, P)], out[:, a.s]).then_inc(stored[a.s], 16)

                for s in range(2):
                    sp.sem_inc(stored[s], 16)
                load(Tile(0, 0, 0))
                sp.dma_start(ident[:], D["ident"][:]).then_inc(const_in, 16)
                sp.dma_start(gain[:], D["g_ple"].partition_broadcast(P)).then_inc(const_in, 16)
                sp.dma_start(gain_final[:], D["g_final"].partition_broadcast(P)).then_inc(const_in, 16)
                for g in range(G):
                    sp.wait_ge(S["w_lo"], g + START)
                    sp.dma_start(w_raw[:], D["w_ple_gate"][:, g * GROUP:(g + 1) * GROUP].rearrange(
                        "(c p) n -> p c n", p=P)).then_inc(w_in, 16)
                    if g == 0:
                        sp.dma_start(e_raw[:], D["w_ple_proj"].rearrange("(c p) n -> p c n", p=P)).then_inc(e_in, 16)
                        load(Tile(0, 0, 1))
                        load_again(Tile(0, 0, 0))

                def pair(j, last):
                    for s in range(2):
                        a = Tile(j, j, s)
                        if not last:
                            load(a.next(2))
                        if not (last and s == 1):
                            load_again(a.next(1))
                        store(a)

                one_pass(sp, pair)
                for s in range(2):
                    sp.wait_ge(stored[s], 16 * (PAIRS + 1))

            @block.scalar
            def _(act):
                def split_w(g):
                    act.wait_ge(w_in, 16 * (g + 1))
                    nc.scalar.copy(w_hi[:, g], w_raw[:]).then_inc(S["w_hi"], 1)

                def square(a):
                    act.wait_ge(h_in[a.s], a.j * 16 + 16)
                    act.wait_ge(S["ssq"], a.n + START)
                    nc.scalar.activation(junk[:], h[:, a.s], ACT.Square,
                                         accum_out=ssq[:, a.s:a.s + 1]).then_inc(S["ssq"], 1)

                def hi(a):
                    act.wait_ge(S["emb_acc"], a.n * 2 - 2 + START)
                    for b in range(2):
                        act.wait_ge(S["turn"], a.n * 2 + (b + 1 + START))
                        nc.scalar.copy(xt_hi[:, a.s, 4 * b:4 * b + 4].rearrange("p c t -> p (c t)"),
                                       turned[:, b]).then_inc(S["hi"], 1)
                    act.wait_ge(S["e_turn"], a.n + (1 + START))
                    nc.scalar.copy(et_hi[:, a.s].rearrange("p c t -> p (c t)"), e_turned[:, :PC * P]).then_inc(S["e_hi"], 1)

                def sigmoid(a):
                    for g in range(G):
                        act.wait_ge(S["gate_acc"], a.n * 2 + (g + 1 + START))
                        act.wait_ge(S["gated"], a.n * 2 + (g - 1 + START))
                        nc.scalar.activation(gate[:, g], gate_acc[:, g], ACT.Sigmoid).then_inc(S["gate"], 1)

                def square2(a):
                    act.wait_ge(S["h3"], a.n * 2 + (2 + START))
                    act.wait_ge(S["ssq2"], a.n + START)
                    nc.scalar.activation(junk2[:], h3[:, a.s], ACT.Square,
                                         accum_out=ssq2[:, a.s:a.s + 1]).then_inc(S["ssq2"], 1)

                for name in "w_hi e_whi ssq hi e_hi gate ssq2".split():
                    act.sem_inc(S[name], START)
                square(Tile(0, 0, 0))
                split_w(0)
                hi(Tile(0, 0, 0))
                act.wait_ge(e_in, 16)
                nc.scalar.copy(e_hi[:], e_raw[:]).then_inc(S["e_whi"], 1)
                split_w(1)
                square(Tile(0, 0, 1))

                def pair(j, last):
                    for s in range(2):
                        a = Tile(j, j, s)
                        if not (last and s == 1):
                            hi(a.next(1))
                        if not last:
                            square(a.next(2))
                        sigmoid(a)
                        square2(a)

                one_pass(act, pair)

            @block.vector
            def _(dve):
                def split_w(g):
                    dve.wait_ge(S["w_hi"], g + 1 + START)
                    nc.vector.tensor_tensor(w_lo[:, g], w_raw[:], w_hi[:, g].bitcast(F32),
                                            ALU.subtract).then_inc(S["w_lo"], 1)

                def normalise(a):
                    v = slice(a.s, a.s + 1)
                    dve.wait_ge(S["ssq"], a.n + (1 + START))
                    nc.vector.tensor_scalar(mean[:, v], ssq[:, v], 1.0 / DM, NORM_EPS,
                                            ALU.mult, ALU.add).then_inc(S["mean"], 1)
                    dve.wait_ge(S["rstd"], a.n + (1 + START))
                    dve.wait_ge(S["turn"], a.n * 2 - 2 + START)
                    nc.vector.scalar_tensor_tensor(out=hn[:, a.s], in0=h[:, a.s], scalar=rstd[:, v], in1=gain[:],
                                                   op0=ALU.mult, op1=ALU.mult).then_inc(S["hn"], 1)

                def lo(a):
                    for b in range(2):
                        dve.wait_ge(S["hi"], a.n * 2 + (b + 1 + START))
                        view = lambda t: t[:, a.s, 4 * b:4 * b + 4].rearrange("p c t -> p (c t)")
                        nc.vector.tensor_tensor(view(xt_lo), turned[:, b], view(xt_hi).bitcast(F32),
                                                ALU.subtract).then_inc(S["lo"], 1)
                    dve.wait_ge(S["e_hi"], a.n + (1 + START))
                    view = lambda t: t[:, a.s].rearrange("p c t -> p (c t)")
                    nc.vector.tensor_tensor(view(et_lo), e_turned[:, :PC * P], view(et_hi).bitcast(F32),
                                            ALU.subtract).then_inc(S["e_lo"], 1)

                def gate_in(a):
                    for g in range(G):
                        dve.wait_ge(S["gate"], a.n * 2 + (g + 1 + START))
                        dve.wait_ge(S["emb_acc"], a.n * 2 + (g + 1 + START))
                        dve.wait_ge(S["h3"], a.n * 2 + (g - 1 + START))
                        nc.vector.tensor_tensor(gated[:, g], emb_acc[:, g], gate[:, g], ALU.mult).then_inc(S["gated"], 1)

                def finish(a):
                    v = slice(a.s, a.s + 1)
                    dve.wait_ge(S["ssq2"], a.n + (1 + START))
                    nc.vector.tensor_scalar(mean2[:, v], ssq2[:, v], 1.0 / DM, NORM_EPS,
                                            ALU.mult, ALU.add).then_inc(S["mean2"], 1)
                    dve.wait_ge(S["rstd2"], a.n + (1 + START))
                    dve.wait_ge(stored[a.s], a.j * 16 + 16)
                    nc.vector.scalar_tensor_tensor(out=out[:, a.s], in0=h3[:, a.s], scalar=rstd2[:, v],
                                                   in1=gain_final[:], op0=ALU.mult, op1=ALU.mult).then_inc(S["out"], 1)

                for name in "w_lo e_wlo mean hn lo e_lo gated mean2 out".split():
                    dve.sem_inc(S[name], START)
                dve.wait_ge(const_in, 48)
                normalise(Tile(0, 0, 0))
                split_w(0)
                lo(Tile(0, 0, 0))
                dve.wait_ge(S["e_whi"], 1 + START)
                nc.vector.tensor_tensor(e_lo[:], e_raw[:], e_hi[:].bitcast(F32), ALU.subtract).then_inc(S["e_wlo"], 1)
                split_w(1)
                normalise(Tile(0, 0, 1))

                def pair(j, last):
                    for s in range(2):
                        a = Tile(j, j, s)
                        if not (last and s == 1):
                            lo(a.next(1))
                        if not last:
                            normalise(a.next(2))
                        gate_in(a)
                        finish(a)

                one_pass(dve, pair)

            @block.gpsimd
            def _(pool):
                def root(a):
                    v = slice(a.s, a.s + 1)
                    pool.wait_ge(S["mean"], a.n + (1 + START))
                    nc.gpsimd.tensor_tensor(rstd[:, v], mean[:, v], half[:], ALU.pow).then_inc(S["rstd"], 1)

                def add(a):
                    pool.wait_ge(res_in[a.s], a.j * 16 + 16)
                    for g in range(G):
                        pool.wait_ge(S["gated"], a.n * 2 + (g + 1 + START))
                        if g == 0:
                            pool.wait_ge(S["out"], a.n - 1 + START)
                        cols = slice(g * GROUP, (g + 1) * GROUP)
                        nc.gpsimd.tensor_tensor(h3[:, a.s, cols], res[:, a.s, cols], gated[:, g],
                                                ALU.add).then_inc(S["h3"], 1)

                def root2(a):
                    v = slice(a.s, a.s + 1)
                    pool.wait_ge(S["mean2"], a.n + (1 + START))
                    nc.gpsimd.tensor_tensor(rstd2[:, v], mean2[:, v], half[:], ALU.pow).then_inc(S["rstd2"], 1)

                for name in "rstd h3 rstd2".split():
                    pool.sem_inc(S[name], START)
                nc.gpsimd.memset(half[:], -0.5).then_inc(half_set, 1)
                pool.wait_ge(half_set, 1)
                root(Tile(0, 0, 0))
                root(Tile(0, 0, 1))

                def pair(j, last):
                    for s in range(2):
                        a = Tile(j, j, s)
                        if not last:
                            root(a.next(2))
                        add(a)
                        root2(a)

                one_pass(pool, pair)

            @block.tensor
            def _(pe):
                def turn(a):
                    pe.wait_ge(S["hn"], a.n + (1 + START))
                    for b in range(2):
                        pe.wait_ge(S["lo"], a.n * 2 + (b - 1 + START))
                        for c in range(4):
                            ins = nc.tensor.transpose(turned[:, b, c * P:(c + 1) * P],
                                                      hn[:, a.s, (4 * b + c) * P:(4 * b + c + 1) * P], ident[:])
                        ins.then_inc(S["turn"], 1)
                    pe.wait_ge(emb_in[a.s], a.j * 16 + 16)
                    pe.wait_ge(S["e_lo"], a.n + START)
                    for c in range(PC):
                        ins = nc.tensor.transpose(e_turned[:, c * P:(c + 1) * P], emb[:, a.s, c * P:(c + 1) * P], ident[:])
                    ins.then_inc(S["e_turn"], 1)

                def products(a):
                    pe.wait_ge(S["lo"], a.n * 2 + (2 + START))
                    for g in range(G):
                        pe.wait_ge(S["w_lo"], g + 1 + START)
                        pe.wait_ge(S["gate"], a.n * 2 + (g - 1 + START))
                        for c in range(KC):
                            ins = matmul3(nc, gate_acc[:, g], xt_hi[:, a.s, c], xt_lo[:, a.s, c],
                                          w_hi[:, g, c], w_lo[:, g, c], c == 0, c == KC - 1)
                        ins.then_inc(S["gate_acc"], 1)
                    pe.wait_ge(S["e_wlo"], 1 + START)
                    pe.wait_ge(S["e_lo"], a.n + (1 + START))
                    for g in range(G):
                        pe.wait_ge(S["gated"], a.n * 2 + (g - 1 + START))
                        cols = slice(g * GROUP, (g + 1) * GROUP)
                        for c in range(PC):
                            ins = matmul3(nc, emb_acc[:, g], et_hi[:, a.s, c], et_lo[:, a.s, c],
                                          e_hi[:, c, cols], e_lo[:, c, cols], c == 0, c == PC - 1)
                        ins.then_inc(S["emb_acc"], 1)

                for name in "turn e_turn gate_acc emb_acc".split():
                    pe.sem_inc(S[name], START)
                pe.wait_ge(const_in, 48)
                turn(Tile(0, 0, 0))

                def pair(j, last):
                    for s in range(2):
                        a = Tile(j, j, s)
                        if not (last and s == 1):
                            turn(a.next(1))
                        products(a)

                one_pass(pe, pair)


PHASES = (project_phase, differential_phase, dilated_phase, mix_phase, mlp_phase, gate_phase)


def build(nc, dram):
    for phase in PHASES:
        kit = Kit(nc, dram)
        phase(kit)
        nc.all_engine_barrier()
        nc.clear_and_free_semaphores(kit.sems)
        nc.all_engine_barrier()



def shape_constants():
    inv = (10000.0 ** (-np.arange(0, HD, 2) / HD)).astype(np.float32)
    ang = np.arange(SEQ, dtype=np.float32)[:, None] * inv[None, :]
    cos, sin = np.cos(ang).astype(np.float32), np.sin(ang).astype(np.float32)
    rot = np.stack([np.concatenate([cos, cos], 1), np.concatenate([-sin, sin], 1)], 1)
    q, i = np.arange(P)[:, None], np.arange(2 * P)[None, :]
    near = np.abs(i - RADIUS - q) <= RADIUS
    kinds = (near & (i >= RADIUS), near, near & (i < P + RADIUS),
             near & (i >= RADIUS) & (i < P + RADIUS))
    masks = np.where(np.stack(kinds, 1), 0.0, NEG)
    return {"masks": np.ascontiguousarray(masks, np.float32), "rot": np.ascontiguousarray(rot, np.float32), "ident": np.eye(P, dtype=np.float32)}


INPUTS = {
    "x": (SEQ, DM), "p": (SEQ, D_PLE), "w_in": (DM, 6 * GROUP), "w_out": (DM, DM), "g_mix": (DM,),
    "lambda_q1": (1, HD), "lambda_k1": (1, HD), "lambda_q2": (1, HD), "lambda_k2": (1, HD),
    "g_subln": (2 * HD,), "g_mlp": (DM,), "w_up": (DM, D_FF), "w_down": (D_FF, DM), "g_ple": (DM,),
    "w_ple_gate": (DM, DM), "w_ple_proj": (D_PLE, DM), "g_final": (DM,),
}


def kernel(**inputs):
    import concourse.bacc as bacc
    from concourse.bass_utils import run_bass_kernel_spmd

    nc = bacc.Bacc("TRN2", target_bir_lowering=False, num_devices=1)
    arrays, dram = {}, {}
    for name, shape in INPUTS.items():
        arrays[name + "_dram"] = np.ascontiguousarray(np.asarray(inputs[name]).reshape(shape))
    for name, a in shape_constants().items():
        arrays[name + "_dram"] = a
    for name, a in arrays.items():
        dram[name[:-5]] = nc.dram_tensor(name, a.shape, F32, kind="ExternalInput").ap()
    dram["out"] = nc.dram_tensor("out_dram", (SEQ, DM), F32, kind="ExternalOutput").ap()
    for name, shape, dt in [
        ("qk", (2, 2, SEQ, MAPS, 2, HD), F32),
        ("v", (2, SEQ, 2 * GROUP), F32),
        ("od", (SEQ, GROUP), F32),
        ("nd", (len(PATTERNS), SEQ, MAPS, HD), F32),
        ("md", (len(PATTERNS), SEQ, MAPS, 2), F32),
        ("h", (SEQ, DM), F32),
        ("h2", (SEQ, DM), F32),
        ("xt_hi", (TILES, P, KC, P), F32),
        ("xt_lo", (TILES, P, KC, P), F32),
    ]:
        dram[name] = nc.dram_tensor("s_" + name, shape, dt).ap()
    build(nc, dram)
    result = run_bass_kernel_spmd(nc, [arrays], core_ids=[0])
    return result.results[0]["out_dram"].reshape(1, SEQ, DM)
```

```python
from contextlib import ExitStack

import numpy as np
import concourse.bass as bass
from concourse import mybir

P = 128
SEQ = 2048
DM = 1024
TILES = SEQ // P
PAIRS = TILES // 2
KC = DM // P
HD = 64
GROUP = 512
MAPS = GROUP // HD
D_FF = 4 * DM
D_PLE = 256
NORM_EPS = 1e-6
SUBLN_EPS = 1e-5
SCALE = HD ** -0.5
NEG = -1e30
PATTERNS = ((128, 1), (512, 4), (2048, 16))
RADIUS = 64
LAM_INIT = 0.8 - 0.6 * 1.0
START = 24

ALU = mybir.AluOpType
ACT = mybir.ActivationFunctionType
F32 = mybir.dt.float32
F32R = mybir.dt.float32r
AX = mybir.AxisListType


class Kit:

    def __init__(self, nc, dram):
        self.nc, self.dram, self.sems = nc, dram, []

    def sem(self, name):
        self.sems.append(self.nc.alloc_semaphore(name=name))
        return self.sems[-1]

    def sem_pair(self, name):
        return [self.sem(f"{name}{i}") for i in range(2)]


class Tile:

    def __init__(self, q, j, s):
        self.q, self.j, self.s = q, j, s
        self.n = q * 2 + s
        self.t = j * 2 + s

    def next(self, k):
        s = (self.s + k) % 2
        up = 1 if self.s + k >= 2 else 0
        j = self.j + up
        if isinstance(j, int) and j == PAIRS:
            j = 0
        return Tile(self.q + up, j, s)

    def before(self):
        return Tile(self.q, self.j, 0) if self.s else Tile(self.q - 1, self.j - 1, 1)


def matmul3(nc, out, lhs_hi, lhs_lo, rhs_hi, rhs_lo, first, last):
    nc.tensor.matmul(out, lhs_hi, rhs_hi, start=first, stop=False)
    nc.tensor.matmul(out, lhs_hi, rhs_lo, start=False, stop=False)
    return nc.tensor.matmul(out, lhs_lo, rhs_hi, start=False, stop=last)


def project_phase(kit):
    nc, D = kit.nc, kit.dram
    KINDS, G = 2, 3
    with ExitStack() as mem:
        sb = lambda name, shape, dt=F32: mem.enter_context(nc.sbuf_tensor("a_" + name, shape, dt))
        ps = lambda name, shape: mem.enter_context(nc.psum_tensor("a_" + name, shape, F32))
        w_raw = sb("w_raw", [P, 2, KC, GROUP])
        w_hi = sb("w_hi", [P, G, KC, GROUP], F32R)
        w_lo = sb("w_lo", [P, G, KC, GROUP], F32R)
        gain = sb("gain", [P, DM])
        ident = sb("ident", [P, P])
        x = sb("x", [P, 2, DM])
        rot = sb("rot", [P, 2, 2, HD])
        xn = sb("xn", [P, 2, DM])
        junk = sb("junk", [P, DM])
        ssq = sb("ssq", [P, 2])
        mean = sb("mean", [P, 2])
        rstd = sb("rstd", [P, 2])
        half = sb("half", [P, 1])
        xt_hi = sb("xt_hi", [P, 2, KC, P], F32R)
        xt_lo = sb("xt_lo", [P, 2, KC, P], F32R)
        raw = sb("raw", [P, 2, GROUP])
        t_cos = sb("t_cos", [P, 2, GROUP])
        t_sin = sb("t_sin", [P, 2, GROUP])
        out = sb("out", [P, 2, 2, GROUP])
        v_out = sb("v_out", [P, 2, 2, GROUP], F32R)
        turned = ps("turned", [P, 2, 4 * P])
        acc = ps("acc", [P, 2, G, GROUP])

        const_in, half_set = kit.sem("a_const_in"), kit.sem("a_half_set")
        w_in, x_in, rot_in, stored = (kit.sem_pair("a_" + s) for s in ("w_in", "x_in", "rot_in", "stored"))
        w_hi_done, w_lo_done, w_used = kit.sem("a_w_hi"), kit.sem("a_w_lo"), kit.sem("a_w_used")
        ssq_done, mean_done, rstd_done, xn_done = (kit.sem("a_" + s) for s in ("ssq", "mean", "rstd", "xn"))
        turned_done, hi_done, lo_done = (kit.sem("a_" + s) for s in ("turned", "hi", "lo"))
        acc_done, acc_out = kit.sem("a_acc"), kit.sem("a_acc_out")
        v_lo_done = kit.sem("a_v_lo")
        cos_done, sin_done, rope_done = (kit.sem("a_" + s) for s in ("cos", "sin", "rope"))
        STORES = 6 * 16

        def passes(eng, pair, between):
            for kind in range(KINDS):
                with eng.Fori(0, PAIRS - 1) as i:
                    pair(kind, i + kind * PAIRS, i, False)
                pair(kind, kind * PAIRS + PAIRS - 1, PAIRS - 1, kind == KINDS - 1)
                between(kind)

        with nc.Block() as block:

            @block.sync
            def _(sp):
                def load_w(n):
                    if n >= 2:
                        sp.wait_ge(w_lo_done, n - 1 + START)
                    sp.dma_start(w_raw[:, n % 2], D["w_in"][:, n * GROUP:(n + 1) * GROUP].rearrange(
                        "(c p) n -> p c n", p=P)).then_inc(w_in[n % 2], 16)

                def load_x(a):
                    sp.wait_ge(xn_done, a.n - 1 + START)
                    sp.dma_start(x[:, a.s], D["x"][bass.ts(a.t, P), :]).then_inc(x_in[a.s], 16)

                def load_rot(a):
                    sp.wait_ge(rope_done, a.n * 2 - 2 + START)
                    sp.dma_start(rot[:, a.s], D["rot"][bass.ts(a.t, P)]).then_inc(rot_in[a.s], 16)

                def store(kind, a):
                    for g in range(2):
                        sp.wait_ge(rope_done, a.n * 2 + (g + 1 + START))
                        for dup in range(2):
                            sp.dma_start(D["qk"][kind, g, bass.ts(a.t, P), :, dup],
                                         out[:, a.s, g].rearrange("p (m d) -> p m d", d=HD)).then_inc(stored[a.s], 16)
                    sp.wait_ge(v_lo_done, a.n + (1 + START))
                    d = (P, HD)[kind]
                    for u in range(2):
                        sp.dma_start(D["v"][kind, bass.ts(a.t, P)].rearrange("p (h u d) -> p h u d", u=2, d=d)[:, :, u],
                                     v_out[:, a.s, u].bitcast(F32).rearrange("p (h d) -> p h d", d=d)
                                     ).then_inc(stored[a.s], 16)

                for s in range(2):
                    sp.sem_inc(stored[s], STORES)
                sp.dma_start(gain[:], D["g_mix"].partition_broadcast(P)).then_inc(const_in, 16)
                sp.dma_start(ident[:], D["ident"][:]).then_inc(const_in, 16)
                load_x(Tile(0, 0, 0))
                load_w(0)
                load_x(Tile(0, 0, 1))
                load_rot(Tile(0, 0, 0))
                for n in range(1, G + 2):
                    load_w(n)

                def pair(kind, q, j, last):
                    for s in range(2):
                        a = Tile(q, j, s)
                        if not last:
                            load_x(a.next(2))
                        if not (last and s == 1):
                            load_rot(a.next(1))
                        store(kind, a)

                passes(sp, pair, lambda kind: load_w(G + 2) if kind == 0 else None)
                for s in range(2):
                    sp.wait_ge(stored[s], STORES * (KINDS * PAIRS + 1))

            @block.scalar
            def _(act):
                def split_w(n):
                    act.wait_ge(w_in[n % 2], 16 * (n // 2 + 1))
                    if n >= G:
                        act.wait_ge(acc_done, (TILES - 1) * G + n - G + 1 + START)
                    nc.scalar.copy(w_hi[:, n % G], w_raw[:, n % 2]).then_inc(w_hi_done, 1)

                def square(a):
                    act.wait_ge(x_in[a.s], a.q * 16 + 16)
                    act.wait_ge(ssq_done, a.n + START)
                    nc.scalar.activation(junk[:], x[:, a.s], ACT.Square,
                                         accum_out=ssq[:, a.s:a.s + 1]).then_inc(ssq_done, 1)

                def hi(a):
                    act.wait_ge(acc_done, a.n * 3 - 3 + START)
                    for b in range(2):
                        act.wait_ge(turned_done, a.n * 2 + (b + 1 + START))
                        nc.scalar.copy(xt_hi[:, a.s, 4 * b:4 * b + 4].rearrange("p c t -> p (c t)"),
                                       turned[:, b]).then_inc(hi_done, 1)

                def evacuate(a):
                    for g in range(2):
                        act.wait_ge(acc_done, a.n * 3 + (g + 1 + START))
                        act.wait_ge(rope_done, a.n * 2 + (g - 1 + START))
                        nc.scalar.copy(raw[:, g], acc[:, a.s, g]).then_inc(acc_out, 1)
                    act.wait_ge(acc_done, a.n * 3 + (3 + START))
                    act.wait_ge(stored[a.s], a.q * STORES + STORES)
                    nc.scalar.copy(v_out[:, a.s, 0], acc[:, a.s, 2]).then_inc(acc_out, 1)

                def pair(kind, q, j, last):
                    for s in range(2):
                        a = Tile(q, j, s)
                        if not (last and s == 1):
                            hi(a.next(1))
                        if not last:
                            square(a.next(2))
                        evacuate(a)

                for step in (ssq_done, hi_done, w_hi_done, acc_out):
                    act.sem_inc(step, START)
                square(Tile(0, 0, 0))
                square(Tile(0, 0, 1))
                split_w(0)
                hi(Tile(0, 0, 0))
                split_w(1)
                split_w(2)
                passes(act, pair, lambda kind: [split_w(n) for n in range(G, 2 * G)] if kind == 0 else None)

            @block.vector
            def _(dve):
                def split_w(n):
                    dve.wait_ge(w_hi_done, n + 1 + START)
                    nc.vector.tensor_tensor(w_lo[:, n % G], w_raw[:, n % 2], w_hi[:, n % G].bitcast(F32),
                                            ALU.subtract).then_inc(w_lo_done, 1)

                def normalise(a):
                    v = slice(a.s, a.s + 1)
                    dve.wait_ge(ssq_done, a.n + (1 + START))
                    nc.vector.tensor_scalar(mean[:, v], ssq[:, v], 1.0 / DM, NORM_EPS,
                                            ALU.mult, ALU.add).then_inc(mean_done, 1)
                    dve.wait_ge(rstd_done, a.n + (1 + START))
                    dve.wait_ge(turned_done, a.n * 2 + (START - 2))
                    nc.vector.scalar_tensor_tensor(out=xn[:, a.s], in0=x[:, a.s], scalar=rstd[:, v], in1=gain[:],
                                                   op0=ALU.mult, op1=ALU.mult).then_inc(xn_done, 1)

                def lo(a):
                    for b in range(2):
                        dve.wait_ge(hi_done, a.n * 2 + (b + 1 + START))
                        nc.vector.tensor_tensor(
                            xt_lo[:, a.s, 4 * b:4 * b + 4].rearrange("p c t -> p (c t)"), turned[:, b],
                            xt_hi[:, a.s, 4 * b:4 * b + 4].rearrange("p c t -> p (c t)").bitcast(F32),
                            ALU.subtract).then_inc(lo_done, 1)

                def rotate(a):
                    dve.wait_ge(rot_in[a.s], a.q * 16 + 16)
                    for g in range(2):
                        view = lambda t: t.rearrange("p (m d) -> p m d", d=HD)
                        dve.wait_ge(acc_out, a.n * 3 + (g + 1 + START))
                        nc.vector.tensor_tensor(view(t_cos[:, g]), view(raw[:, g]),
                                                rot[:, a.s, 0].unsqueeze(1).to_broadcast([P, MAPS, HD]),
                                                ALU.mult).then_inc(cos_done, 1)
                        dve.wait_ge(cos_done, a.n * 2 + (g + 1 + START))
                        dve.wait_ge(sin_done, a.n * 4 + (2 * g + 2 + START))
                        dve.wait_ge(stored[a.s], a.q * STORES + STORES)
                        nc.vector.tensor_tensor(out[:, a.s, g], t_cos[:, g], t_sin[:, g],
                                                ALU.add).then_inc(rope_done, 1)

                def split_v(a):
                    dve.wait_ge(acc_out, a.n * 3 + (3 + START))
                    nc.vector.tensor_tensor(v_out[:, a.s, 1], acc[:, a.s, 2], v_out[:, a.s, 0].bitcast(F32),
                                            ALU.subtract).then_inc(v_lo_done, 1)

                for step in (mean_done, xn_done, w_lo_done, lo_done, cos_done, rope_done, v_lo_done):
                    dve.sem_inc(step, START)
                dve.wait_ge(const_in, 32)
                normalise(Tile(0, 0, 0))
                normalise(Tile(0, 0, 1))
                split_w(0)
                lo(Tile(0, 0, 0))
                split_w(1)
                split_w(2)

                def pair(kind, q, j, last):
                    for s in range(2):
                        a = Tile(q, j, s)
                        if not (last and s == 1):
                            lo(a.next(1))
                        if not last:
                            normalise(a.next(2))
                        rotate(a)
                        split_v(a)

                passes(dve, pair, lambda kind: [split_w(n) for n in range(G, 2 * G)] if kind == 0 else None)

            @block.gpsimd
            def _(pool):
                def rotate(a):
                    pool.wait_ge(rot_in[a.s], a.q * 16 + 16)
                    for g in range(2):
                        pool.wait_ge(acc_out, a.n * 3 + (g + 1 + START))
                        pool.wait_ge(rope_done, a.n * 2 + (g - 1 + START))
                        half = lambda t, h: t.rearrange("p (m h d) -> p m h d", h=2, d=HD // 2)[:, :, h]
                        for h in range(2):
                            nc.gpsimd.tensor_tensor(
                                half(t_sin[:, g], h), half(raw[:, g], 1 - h),
                                rot[:, a.s, 1, h * 32:h * 32 + 32].unsqueeze(1).to_broadcast([P, MAPS, HD // 2]),
                                ALU.mult).then_inc(sin_done, 1)

                def root(a):
                    v = slice(a.s, a.s + 1)
                    pool.wait_ge(mean_done, a.n + (1 + START))
                    nc.gpsimd.tensor_tensor(rstd[:, v], mean[:, v], half[:], ALU.pow).then_inc(rstd_done, 1)

                def pair(kind, q, j, last):
                    for s in range(2):
                        a = Tile(q, j, s)
                        if not last:
                            root(a.next(2))
                        rotate(a)

                for step in (rstd_done, sin_done):
                    pool.sem_inc(step, START)
                nc.gpsimd.memset(half[:], -0.5).then_inc(half_set, 1)
                pool.wait_ge(half_set, 1)
                root(Tile(0, 0, 0))
                root(Tile(0, 0, 1))
                passes(pool, pair, lambda kind: None)

            @block.tensor
            def _(pe):
                def turn(a):
                    pe.wait_ge(xn_done, a.n + (1 + START))
                    for b in range(2):
                        pe.wait_ge(lo_done, a.n * 2 + (b - 1 + START))
                        for c in range(4):
                            ins = nc.tensor.transpose(turned[:, b, c * P:(c + 1) * P],
                                                      xn[:, a.s, (4 * b + c) * P:(4 * b + c + 1) * P], ident[:])
                        ins.then_inc(turned_done, 1)

                def project(kind, a):
                    pe.wait_ge(lo_done, a.n * 2 + (2 + START))
                    for g in range(G):
                        pe.wait_ge(w_lo_done, kind * G + g + 1 + START)
                        if g == 2:
                            pe.wait_ge(v_lo_done, a.n - 1 + START)
                        else:
                            pe.wait_ge(acc_out, a.n * 3 + (g - 5 + START))
                        for c in range(KC):
                            ins = matmul3(nc, acc[:, a.s, g], xt_hi[:, a.s, c], xt_lo[:, a.s, c],
                                          w_hi[:, g, c], w_lo[:, g, c], c == 0, c == KC - 1)
                        ins.then_inc(acc_done, 1)

                def pair(kind, q, j, last):
                    for s in range(2):
                        a = Tile(q, j, s)
                        if not (last and s == 1):
                            turn(a.next(1))
                        project(kind, a)

                for step in (turned_done, acc_done):
                    pe.sem_inc(step, START)
                pe.wait_ge(const_in, 32)
                turn(Tile(0, 0, 0))
                passes(pe, pair, lambda kind: None)


def differential_phase(kit):
    nc, D = kit.nc, kit.dram
    HEADS, VD, KT = MAPS // 2, 2 * HD, SEQ // P
    HALF = SEQ // 2
    with ExitStack() as mem:
        sb = lambda name, shape, dt=F32: mem.enter_context(nc.sbuf_tensor("c_" + name, shape, dt))
        ps = lambda name, shape: mem.enter_context(nc.psum_tensor("c_" + name, shape, F32))
        ident = sb("ident", [P, P])
        lam_in = sb("lam_in", [P, 4, HD])
        lam_prod = sb("lam_prod", [P, 2, HD])
        lam_dot = sb("lam_dot", [P, 2])
        lam_exp = sb("lam_exp", [P, 2])
        neg_lam = sb("neg_lam", [P, 1])
        gain_in = sb("gain_in", [P, VD])
        gain = sb("gain", [P, VD])
        half = sb("half", [P, 1])
        k_raw = sb("k_raw", [P, KT, 2, P])
        kt_hi = sb("kt_hi", [P, 2, SEQ], F32R)
        kt_lo = sb("kt_lo", [P, 2, SEQ], F32R)
        v_hl = sb("v_hl", [P, KT, 2, VD], F32R)
        q_raw = sb("q_raw", [P, 2, 2, P])
        qs = sb("qs", [P, 2, 2, P], F32R)
        mx = sb("mx", [P, 2])
        neg_max = sb("neg_max", [P, 2, 2])
        e = sb("e", [P, 2, 2, SEQ])
        sums = sb("sums", [P, 2, 2, 2])
        den = sb("den", [P, 2])
        rec = sb("rec", [P, 2])
        rec0 = sb("rec0", [P, 2])
        coef = sb("coef", [P, 1])
        a_row = sb("a_row", [P, 2, SEQ])
        at_hi = sb("at_hi", [P, 2, KT, P], F32R)
        at_lo = sb("at_lo", [P, 2, KT, P], F32R)
        o_part = sb("o_part", [P, VD])
        o = sb("o", [P, VD])
        o_junk = sb("o_junk", [P, VD])
        o_ssq = sb("o_ssq", [P, 1])
        o_part_mean = sb("o_part_mean", [P, 1])
        o_mean = sb("o_mean", [P, 1])
        inv_dim, eps = sb("inv_dim", [P, 1]), sb("eps", [P, 1])
        o_rstd = sb("o_rstd", [P, 1])
        o_unit = sb("o_unit", [P, VD])
        out = sb("out", [P, 2, VD])
        scores = ps("scores", [P, 4, 512])
        turned = ps("turned", [P, 2, 512])
        pv = ps("pv", [P, 512])
        q_turned = ps("q_turned", [P, 512])

        const_in, consts, gain_done = kit.sem("c_const_in"), kit.sem("c_consts"), kit.sem("c_gain")
        lam_dots, half_set = kit.sem("c_lam_dots"), kit.sem("c_half_set")
        loads_begun = kit.sem("c_loads_begun")
        k_in, v_in, q_in, stored = kit.sem("c_k_in"), kit.sem("c_v_in"), kit.sem_pair("c_q_in"), kit.sem_pair("c_stored")
        names = ("kt_turned k_hi k_lo q_turn q_hi q_lo scored mx negmax exp den rec coef kept a a_turned "
                 "a_hi a_lo a_lo2 pv part o ssq scaled mean rstd unit out")
        S = {name: kit.sem("c_" + name) for name in names.split()}

        def steps(eng, head_start, step, head_end):
            with eng.Fori(0, HEADS) as h:
                one_head(eng, h, head_start, step, head_end)

        def one_head(eng, h, head_start, step, head_end):
            base = h * TILES
            head_start(h)
            for t in range(3):
                step(h, base + t, t, t % 2, 3, t)
            with eng.Fori(0, PAIRS - 3) as i:
                for k in range(3, 5):
                    step(h, base + (i * 2 + k), i * 2 + k, k % 2, 3, 3)
            for t in range(TILES - 3, TILES):
                step(h, base + t, t, t % 2, TILES - 1 - t, 3)
            head_end(h, base + (TILES - 1))

        with nc.Block() as block:

            @block.sync
            def _(sp):
                def load_q(h, n, t, s):
                    sp.wait_ge(S["q_turn"], n - 1 + START)
                    sp.sem_inc(loads_begun, 1)
                    sp.dma_start(q_raw[:, s], D["qk"][0, 0, bass.ts(t, P), bass.ts(h, 2)].rearrange(
                        "p m u d -> p m (u d)")).then_inc(q_in[s], 16)

                def load_k(h):
                    sp.wait_ge(S["kt_turned"], h * 8 + START)
                    sp.sem_inc(loads_begun, 1)
                    sp.dma_start(k_raw[:], D["qk"][0, 1, :, bass.ts(h, 2)].rearrange(
                        "(t p) m u d -> p t m (u d)", p=P)).then_inc(k_in, 16)

                def load_v(h):
                    sp.wait_ge(S["pv"], h * TILES + START)
                    sp.sem_inc(loads_begun, 1)
                    sp.dma_start(v_hl[:].rearrange("p t u d -> p t (u d)").bitcast(F32),
                                 D["v"][0, :, bass.ts(h, 2 * VD)].rearrange("(t p) d -> p t d", p=P)).then_inc(v_in, 16)

                def store(h, n, t, s):
                    sp.wait_ge(S["out"], n + (1 + START))
                    sp.dma_start(D["od"][bass.ts(t, P), bass.ts(h, VD)], out[:, s]).then_inc(stored[s], 16)

                def step(h, n, t, s, ahead, behind):
                    if ahead == 3:
                        load_q(h, n + 3, t + 3, 1 - s)
                    elif ahead and not isinstance(h, int):
                        load_q(h + 1, n + 3, 2 - ahead, 1 - s)
                    if behind == 3:
                        store(h, n - 3, t - 3, 1 - s)

                def head_end(h, n):
                    if not isinstance(h, int):
                        load_v(h + 1)
                    store(h, n - 2, TILES - 3, 1)
                    store(h, n - 1, TILES - 2, 0)
                    store(h, n, TILES - 1, 1)
                    if not isinstance(h, int):
                        load_q(h + 1, n + 3, 2, 0)

                for s in range(2):
                    sp.sem_inc(stored[s], 16)

                sp.dma_start(ident[:], D["ident"][:]).then_inc(const_in, 16)
                for k, name in enumerate(("lambda_q1", "lambda_k1", "lambda_q2", "lambda_k2")):
                    sp.dma_start(lam_in[:, k], D[name][0].partition_broadcast(P)).then_inc(const_in, 16)
                sp.dma_start(gain_in[:], D["g_subln"].partition_broadcast(P)).then_inc(const_in, 16)
                load_k(0)
                load_q(0, 0, 0, 0)
                load_q(0, 1, 1, 1)
                load_q(0, 2, 2, 0)
                load_v(0)
                with sp.Fori(0, HEADS - 1) as h:
                    one_head(sp, h, lambda h: load_k(h + 1), step, head_end)
                one_head(sp, HEADS - 1, lambda h: None, step, head_end)
                for s in range(2):
                    sp.wait_ge(stored[s], 16 * (HEADS * PAIRS + 1))

            @block.scalar
            def _(act):
                def q_hi(n, s):
                    act.wait_ge(S["q_turn"], n + (1 + START))
                    nc.scalar.copy(qs[:, s].rearrange("p m t -> p (m t)"), q_turned[:, :2 * P]).then_inc(S["q_hi"], 1)

                def exp(n, s, m, f):
                    act.wait_ge(S["negmax"], n * 2 + (m + 1 + START))
                    if m == 0 and f == 0:
                        act.wait_ge(S["a"], n - 1 + START)
                    nc.scalar.activation(e[:, s, m, f * HALF:(f + 1) * HALF],
                                         scores[:, 2 * f:2 * f + 2].rearrange("p b k -> p (b k)"), ACT.Exp,
                                         bias=neg_max[:, s, m:m + 1], scale=SCALE,
                                         accum_out=sums[:, s, m, f:f + 1]).then_inc(S["exp"], 1)

                def a_hi(n, s, g):
                    act.wait_ge(S["a_turned"], n * 4 + (g + 1 + START))
                    nc.scalar.copy(at_hi[:, s, 4 * g:4 * g + 4].rearrange("p c t -> p (c t)"),
                                   turned[:, g % 2]).then_inc(S["a_hi"], 1)

                def part(n, s):
                    act.wait_ge(S["pv"], n + (1 + START))
                    act.wait_ge(S["o"], n + START)
                    act.wait_ge(S["kept"], n + (1 + START))
                    nc.scalar.activation(o_part[:], pv[:, VD:2 * VD], ACT.Copy,
                                         scale=rec0[:, s:s + 1]).then_inc(S["part"], 1)

                def square(n):
                    act.wait_ge(S["o"], n + (1 + START))
                    act.wait_ge(S["ssq"], n + START)
                    nc.scalar.activation(o_junk[:], o[:], ACT.Square, accum_out=o_ssq[:]).then_inc(S["ssq"], 1)

                def unit(n):
                    act.wait_ge(S["rstd"], n + (1 + START))
                    act.wait_ge(S["out"], n + START)
                    nc.scalar.activation(o_unit[:], o[:], ACT.Copy, scale=o_rstd[:]).then_inc(S["unit"], 1)

                def head_start(h):
                    for g in range(8):
                        act.wait_ge(S["kt_turned"], h * 8 + (g + 1 + START))
                        nc.scalar.copy(kt_hi[:, g // 4, (g % 4) * 512:(g % 4) * 512 + 512],
                                       scores[:, g % 4]).then_inc(S["k_hi"], 1)
                    q_hi(h * TILES, 0)
                    for m in range(2):
                        if m == 1:
                            q_hi(h * TILES + 1, 1)
                        for f in range(2):
                            exp(h * TILES, 0, m, f)

                def step(h, n, t, s, ahead, behind):
                    if ahead:
                        exp(n + 1, 1 - s, 0, 0)
                        exp(n + 1, 1 - s, 0, 1)
                    if behind >= 3:
                        unit(n - 3)
                    if behind >= 2:
                        part(n - 2, s)
                    if ahead >= 2:
                        q_hi(n + 2, s)
                    a_hi(n, s, 0)
                    a_hi(n, s, 1)
                    if ahead:
                        exp(n + 1, 1 - s, 1, 0)
                        exp(n + 1, 1 - s, 1, 1)
                    a_hi(n, s, 2)
                    a_hi(n, s, 3)
                    if behind >= 2:
                        square(n - 2)

                def head_end(h, n):
                    unit(n - 2)
                    for k, s in ((n - 1, 0), (n, 1)):
                        part(k, s)
                        square(k)
                        unit(k)

                for name in "k_hi q_hi exp a_hi part ssq unit".split():
                    act.sem_inc(S[name], START)
                act.wait_ge(consts, 1)
                nc.scalar.activation(lam_exp[:], lam_dot[:], ACT.Exp).then_inc(consts, 1)
                act.wait_ge(const_in, 96)
                nc.scalar.mul(gain[:], gain_in[:], 1.0 - LAM_INIT).then_inc(gain_done, 1)
                steps(act, head_start, step, head_end)

            @block.vector
            def _(dve):
                def q_lo(n, s):
                    dve.wait_ge(S["q_hi"], n + (1 + START))
                    low = qs[HD:, s].rearrange("p m t -> p (m t)")
                    nc.vector.tensor_tensor(low, q_turned[HD:, :2 * P], low.bitcast(F32),
                                            ALU.subtract).then_inc(S["q_lo"], 1)

                def maximum(n, m, f):
                    dve.wait_ge(S["scored"], n * 4 + (2 * m + f + 1 + START))
                    dve.wait_ge(S["negmax"], n * 2 + (m + START))
                    nc.vector.tensor_reduce(mx[:, f:f + 1], scores[:, 2 * f:2 * f + 2].rearrange("p b k -> p (b k)"),
                                            AX.X, ALU.max).then_inc(S["mx"], 1)

                def negate(n, s, m):
                    dve.wait_ge(S["mx"], n * 4 + (2 * m + 2 + START))
                    nc.vector.tensor_scalar(neg_max[:, s, m:m + 1], mx[:, 0:1], mx[:, 1:2], -SCALE,
                                            ALU.max, ALU.mult).then_inc(S["negmax"], 1)

                def denominators(n, s):
                    dve.wait_ge(S["exp"], n * 4 + (4 + START))
                    dve.wait_ge(S["coef"], n + START)
                    nc.vector.tensor_tensor(den[:], sums[:, s, :, 0], sums[:, s, :, 1], ALU.add).then_inc(S["den"], 1)

                def reciprocals(n, s):
                    dve.wait_ge(S["den"], n + (1 + START))
                    dve.wait_ge(S["kept"], n + START)
                    nc.vector.reciprocal(rec[:], den[:]).then_inc(S["rec"], 1)

                def coefficient(n, s):
                    dve.wait_ge(S["rec"], n + (1 + START))
                    dve.wait_ge(S["a"], n + START)
                    nc.vector.tensor_scalar(coef[:], den[:, 0:1], neg_lam[:], rec[:, 1:2],
                                            ALU.mult, ALU.mult).then_inc(S["coef"], 1)

                def keep(n, s):
                    dve.wait_ge(S["rec"], n + (1 + START))
                    dve.wait_ge(S["part"], n - 1 + START)
                    dve.wait_ge(S["o"], n - 1 + START)
                    nc.vector.tensor_copy(rec0[:, s:s + 1], rec[:, 0:1]).then_inc(S["kept"], 1)

                def combine(n, s):
                    dve.wait_ge(S["coef"], n + (1 + START))
                    dve.wait_ge(S["a_turned"], n * 4 - 4 + START)
                    nc.vector.scalar_tensor_tensor(out=a_row[:, s], in0=e[:, s, 1], scalar=coef[:], in1=e[:, s, 0],
                                                   op0=ALU.mult, op1=ALU.add).then_inc(S["a"], 1)

                def a_lo(n, s, g):
                    dve.wait_ge(S["a_hi"], n * 4 + (g + 1 + START))
                    view = lambda t: t[:, s, 4 * g:4 * g + 4].rearrange("p c t -> p (c t)")
                    nc.vector.tensor_tensor(view(at_lo), turned[:, g % 2], view(at_hi).bitcast(F32),
                                            ALU.subtract).then_inc(S["a_lo" if g < 2 else "a_lo2"], 1)

                def result(n, s):
                    dve.wait_ge(S["part"], n + (1 + START))
                    dve.wait_ge(S["unit"], n + START)
                    nc.vector.scalar_tensor_tensor(out=o[:], in0=pv[:, :VD], scalar=rec0[:, s:s + 1], in1=o_part[:],
                                                   op0=ALU.mult, op1=ALU.add).then_inc(S["o"], 1)

                def head_start(h):
                    for g in range(8):
                        dve.wait_ge(S["k_hi"], h * 8 + (g + 1 + START))
                        cols = slice((g % 4) * 512, (g % 4) * 512 + 512)
                        nc.vector.tensor_tensor(kt_lo[:, g // 4, cols], scores[:, g % 4],
                                                kt_hi[:, g // 4, cols].bitcast(F32), ALU.subtract).then_inc(S["k_lo"], 1)
                    q_lo(h * TILES, 0)
                    for m in range(2):
                        maximum(h * TILES, m, 0)
                        maximum(h * TILES, m, 1)
                        negate(h * TILES, 0, m)
                        if m == 0:
                            q_lo(h * TILES + 1, 1)

                def step(h, n, t, s, ahead, behind):
                    if ahead:
                        maximum(n + 1, 0, 0)
                    denominators(n, s)
                    if behind:
                        a_lo(n - 1, 1 - s, 2)
                    reciprocals(n, s)
                    if ahead:
                        maximum(n + 1, 0, 1)
                    coefficient(n, s)
                    if ahead:
                        negate(n + 1, 1 - s, 0)
                    if behind:
                        a_lo(n - 1, 1 - s, 3)
                    combine(n, s)
                    if ahead:
                        maximum(n + 1, 1, 0)
                        maximum(n + 1, 1, 1)
                        negate(n + 1, 1 - s, 1)
                    a_lo(n, s, 0)
                    if ahead >= 2:
                        q_lo(n + 2, s)
                    a_lo(n, s, 1)
                    if behind >= 2:
                        result(n - 2, s)
                    keep(n, s)

                def head_end(h, n):
                    a_lo(n, 1, 2)
                    a_lo(n, 1, 3)
                    result(n - 1, 0)
                    result(n, 1)

                for name in "k_lo q_lo mx negmax den rec coef kept a a_lo a_lo2 o".split():
                    dve.sem_inc(S[name], START)
                dve.wait_ge(const_in, 96)
                for k in range(2):
                    nc.vector.tensor_tensor_reduce(lam_prod[:, k], lam_in[:, 2 * k], lam_in[:, 2 * k + 1], 1.0, 0.0,
                                                   ALU.mult, ALU.add, lam_dot[:, k:k + 1]).then_inc(lam_dots, 1)
                dve.wait_ge(lam_dots, 2)
                dve.sem_inc(consts, 1)
                dve.wait_ge(consts, 2)
                nc.vector.tensor_scalar(neg_lam[:], lam_exp[:, 1:2], lam_exp[:, 0:1], -LAM_INIT,
                                        ALU.subtract, ALU.add).then_inc(consts, 1)
                dve.wait_ge(consts, 3)
                steps(dve, head_start, step, head_end)

            @block.gpsimd
            def _(pool):
                def root(n):
                    pool.wait_ge(S["ssq"], n + (1 + START))
                    nc.gpsimd.tensor_tensor(o_part_mean[:], o_ssq[:], inv_dim[:], ALU.mult).then_inc(S["scaled"], 1)
                    pool.wait_ge(S["scaled"], n + (1 + START))
                    nc.gpsimd.tensor_tensor(o_mean[:], o_part_mean[:], eps[:], ALU.add).then_inc(S["mean"], 1)
                    pool.wait_ge(S["mean"], n + (1 + START))
                    nc.gpsimd.tensor_tensor(o_rstd[:], o_mean[:], half[:], ALU.pow).then_inc(S["rstd"], 1)

                def finish(n, s):
                    pool.wait_ge(S["unit"], n + (1 + START))
                    pool.wait_ge(stored[s], (n - s) * 8 + 16)
                    nc.gpsimd.tensor_tensor(out[:, s], o_unit[:], gain[:], ALU.mult).then_inc(S["out"], 1)

                def step(h, n, t, s, ahead, behind):
                    if behind >= 3:
                        finish(n - 3, 1 - s)
                    if behind >= 2:
                        root(n - 2)

                def head_end(h, n):
                    finish(n - 2, 1)
                    for k, s in ((n - 1, 0), (n, 1)):
                        root(k)
                        finish(k, s)

                for name in "scaled mean rstd out".split():
                    pool.sem_inc(S[name], START)
                nc.gpsimd.memset(half[:], -0.5).then_inc(half_set, 1)
                nc.gpsimd.memset(inv_dim[:], 1.0 / VD).then_inc(half_set, 1)
                nc.gpsimd.memset(eps[:], SUBLN_EPS).then_inc(half_set, 1)
                pool.wait_ge(half_set, 3)
                pool.wait_ge(gain_done, 1)
                steps(pool, lambda h: None, step, head_end)

            @block.tensor
            def _(pe):
                def turn_q(n, s):
                    pe.wait_ge(q_in[s], (n - s) * 8 + 16)
                    pe.wait_ge(S["q_lo"], n + START)
                    for m in range(2):
                        ins = nc.tensor.transpose(q_turned[:, m * P:(m + 1) * P], q_raw[:, s, m], ident[:])
                    ins.then_inc(S["q_turn"], 1)

                def score(n, s, m):
                    pe.wait_ge(S["q_lo"], n + (1 + START))
                    for b in range(4):
                        if b % 2 == 0:
                            pe.wait_ge(S["exp"], n * 4 + (2 * m - 2 + b // 2 + 1 + START))
                        cols = slice(b * 512, b * 512 + 512)
                        nc.tensor.matmul(scores[:, b], qs[:, s, m], kt_hi[:, m, cols], start=True, stop=False)
                        ins = nc.tensor.matmul(scores[:, b], qs[:, s, m], kt_lo[:, m, cols], start=False, stop=True)
                        if b % 2 == 1:
                            ins.then_inc(S["scored"], 1)

                def turn_a(n, s, g):
                    pe.wait_ge(S["a"], n + (1 + START))
                    if g < 2:
                        pe.wait_ge(S["a_lo2"], n * 2 + (g - 1 + START))
                    else:
                        pe.wait_ge(S["a_lo"], n * 2 + (g - 1 + START))
                    for c in range(4):
                        ins = nc.tensor.transpose(turned[:, g % 2, c * P:(c + 1) * P],
                                                  a_row[:, s, (4 * g + c) * P:(4 * g + c + 1) * P], ident[:])
                    ins.then_inc(S["a_turned"], 1)

                def values(h, n, s, half):
                    if half == 0:
                        pe.wait_ge(v_in, h * 16 + 16)
                        pe.wait_ge(S["o"], n + START)
                    pe.wait_ge(S[("a_lo", "a_lo2")[half]], n * 2 + (2 + START))
                    for c in range(half * KT // 2, (half + 1) * KT // 2):
                        v = v_hl[:, c].rearrange("p u d -> p (u d)")
                        nc.tensor.matmul(pv[:, :2 * VD], at_hi[:, s, c], v, start=(c == 0), stop=False)
                        ins = nc.tensor.matmul(pv[:, :2 * VD], at_lo[:, s, c], v, start=False, stop=(c == KT - 1))
                    if half == 1:
                        ins.then_inc(S["pv"], 1)

                def head_start(h):
                    pe.wait_ge(k_in, h * 16 + 16)
                    for g in range(8):
                        m, b = g // 4, g % 4
                        if g < 4:
                            pe.wait_ge(S["exp"], h * (TILES * 4) + START)
                        else:
                            pe.wait_ge(S["k_lo"], h * 8 + (g - 3 + START))
                        for c in range(4):
                            ins = nc.tensor.transpose(scores[:, b, c * P:(c + 1) * P], k_raw[:, 4 * b + c, m], ident[:])
                        ins.then_inc(S["kt_turned"], 1)
                    turn_q(h * TILES, 0)
                    turn_q(h * TILES + 1, 1)
                    pe.wait_ge(S["k_lo"], h * 8 + (8 + START))
                    score(h * TILES, 0, 0)
                    score(h * TILES, 0, 1)
                    score(h * TILES + 1, 1, 0)

                def step(h, n, t, s, ahead, behind):
                    if behind >= 2:
                        values(h, n - 2, s, 1)
                    if ahead:
                        score(n + 1, 1 - s, 1)
                    if ahead >= 2:
                        turn_q(n + 2, s)
                    turn_a(n, s, 0)
                    turn_a(n, s, 1)
                    turn_a(n, s, 2)
                    if ahead >= 2:
                        score(n + 2, s, 0)
                    turn_a(n, s, 3)
                    if behind:
                        values(h, n - 1, 1 - s, 0)

                def head_end(h, n):
                    values(h, n - 1, 0, 1)
                    values(h, n, 1, 0)
                    values(h, n, 1, 1)

                for name in "kt_turned q_turn scored a_turned pv".split():
                    pe.sem_inc(S[name], START)
                pe.wait_ge(const_in, 96)
                steps(pe, head_start, step, head_end)


def dilated_phase(kit):
    nc, D = kit.nc, kit.dram
    HEADS, NP = MAPS, len(PATTERNS)
    WORK = NP * PAIRS
    EDGE = RADIUS * PATTERNS[1][1]
    KEYS = P + 2 * RADIUS
    SUB = [TILES // d for _, d in PATTERNS]
    CHUNKS = [n + 1 if n > 1 else 1 for n in SUB]
    BASE = [0, CHUNKS[0], CHUNKS[0] + CHUNKS[1] * PATTERNS[1][1]]
    N_CHUNKS = BASE[2] + CHUNKS[2] * PATTERNS[2][1]
    V_LOADS = [16 * (d + 2 if n > 1 else 1) for (_, d), n in zip(PATTERNS, SUB)]
    STORES = [16 * (d if n > 1 else 1) for (_, d), n in zip(PATTERNS, SUB)]
    with ExitStack() as mem:
        sb = lambda name, shape, dt=F32: mem.enter_context(nc.sbuf_tensor("b_" + name, shape, dt))
        ps = lambda name, shape: mem.enter_context(nc.psum_tensor("b_" + name, shape, F32))
        ident = sb("ident", [P, P])
        masks = sb("masks", [P, 4, KEYS])
        raw = sb("raw", [P, 2, TILES, 2 * HD])
        kt = sb("kt", [P, 2, SEQ + 2 * EDGE], F32R)
        qs = sb("qs", [P, SEQ], F32R)
        v_hl = sb("v_hl", [P, N_CHUNKS, 2 * HD], F32R)
        masked = sb("masked", [P, 4, 2, KEYS])
        neg_max = sb("neg_max", [P, 4, 2])
        e = sb("e", [P, 4, 2, KEYS])
        et_hi = sb("et_hi", [P, 2, 4, P], F32R)
        et_lo = sb("et_lo", [P, 2, 4, P], F32R)
        nout = sb("nout", [P, NP, TILES, HD])
        md_head = sb("md_head", [P, NP, TILES, 2])
        md_all = sb("md_all", [P, NP, TILES, HEADS, 2])
        scores = ps("scores", [P, 4, 2, KEYS])
        turned = ps("turned", [P, 2, 4, P])
        pv = ps("pv", [P, 2, 2, 4 * HD])

        const_in, zeroed, raw_in = kit.sem("b_const_in"), kit.sem("b_zeroed"), kit.sem("b_raw_in")
        v_in, stored = ([kit.sem(f"b_{s}{p}") for p in range(NP)] for s in ("v_in", "stored"))
        md_stored = kit.sem("b_md_stored")
        loads_begun, masks_begun = kit.sem("b_loads_begun"), kit.sem("b_masks_begun")
        names = "prep_turn prep_hi prep_lo scored masked negmax exp e_turn e_hi e_lo pv out md"
        S = {name: kit.sem("b_" + name) for name in names.split()}

        MASK, EXP, TURN, VALUES, OUT = 1, 2, 3, 4, 5
        LAST = OUT

        def now(w, lag):
            return lag <= w < WORK + lag

        def pattern(w):
            return w // PAIRS

        def tile_of(w, s):
            t = w % PAIRS * 2 + s
            return t // SUB[pattern(w)], t % SUB[pattern(w)]

        def used(w, t):
            return t if pattern(w) < 2 else t[:, :, :P]

        def heads(eng, prepare, step):
            with eng.Fori(0, HEADS) as h:
                prepare(h)
                for w in range(WORK + LAST):
                    step(h, h * WORK, w)

        with nc.Block() as block:

            @block.sync
            def _(sp):
                def load_raw(h):
                    for g in range(2):
                        sp.dma_start(raw[:, g], D["qk"][1, 1 - g, :, bass.ts(h, 1)].rearrange(
                            "(t p) m u d -> p t (m u d)", p=P)).then_inc(raw_in, 16)

                def load_v(h, p):
                    d, n, b = PATTERNS[p][1], SUB[p], BASE[p]
                    src = D["v"][1, :, bass.ts(h, 2 * HD)].rearrange("(k r) x -> r k x", r=d)
                    dst = v_hl[:, b:b + CHUNKS[p] * d].rearrange("p (r c) x -> p r c x", r=d).bitcast(F32)
                    if n == 1:
                        sp.dma_start(dst[:, :, 0], src.rearrange("r k x -> k r x")).then_inc(v_in[p], 16)
                        return
                    for r in range(d):
                        sp.dma_start(dst[:, r, 1:n], src[r, RADIUS:RADIUS + (n - 1) * P].rearrange(
                            "(c p) x -> p c x", p=P)).then_inc(v_in[p], 16)
                    sp.dma_start(dst[RADIUS:, :, 0], src[:, :RADIUS].rearrange("r k x -> k r x")).then_inc(v_in[p], 16)
                    sp.dma_start(dst[:RADIUS, :, n], src[:, n * P - RADIUS:].rearrange(
                        "r k x -> k r x")).then_inc(v_in[p], 16)

                def by_token(t, p):
                    d, n = PATTERNS[p][1], SUB[p]
                    if n == 1:
                        return [t.rearrange("(k r) x -> k r x", r=d)]
                    return [t.rearrange("(c p r) x -> r p c x", p=P, r=d)[r] for r in range(d)]

                def store(h, p):
                    sp.wait_ge(S["out"], h * WORK + ((p + 1) * PAIRS + START))
                    views = by_token(D["nd"][p].rearrange("s h d -> s (h d)")[:, bass.ts(h, HD)], p)
                    for r, view in enumerate(views):
                        n = TILES // len(views)
                        sp.dma_start(view, nout[:, p, r * n:(r + 1) * n]).then_inc(stored[p], 16)

                for p in range(NP):
                    sp.sem_inc(stored[p], STORES[p])
                sp.dma_start(ident[:], D["ident"][:]).then_inc(const_in, 16)
                load_raw(0)
                sp.dma_start(masks[:], D["masks"][:]).then_inc(const_in, 16)
                for p in range(NP):
                    load_v(0, p)
                with sp.Fori(0, HEADS - 1) as h:
                    sp.wait_ge(S["prep_turn"], h * 8 + (8 + START))
                    sp.sem_inc(loads_begun, 1)
                    load_raw(h + 1)
                    for p in range(NP):
                        store(h, p)
                        sp.wait_ge(S["pv"], h * WORK + ((p + 1) * PAIRS + START))
                        sp.sem_inc(loads_begun, 1)
                        load_v(h + 1, p)
                for p in range(NP):
                    store(HEADS - 1, p)
                sp.wait_ge(S["md"], HEADS + START)
                for p in range(NP):
                    views = by_token(D["md"][p].rearrange("s h c -> s (h c)"), p)
                    for r, view in enumerate(views):
                        n = TILES // len(views)
                        sp.dma_start(view, md_all[:, p, r * n:(r + 1) * n].rearrange("p t h c -> p t (h c)")
                                     ).then_inc(md_stored, 16)
                for p in range(NP):
                    sp.wait_ge(stored[p], STORES[p] * (HEADS + 1))
                sp.wait_ge(md_stored, sum(STORES))

            @block.scalar
            def _(act):
                def prepare(h):
                    for g in range(8):
                        act.wait_ge(S["prep_turn"], h * 8 + (g + 1 + START))
                        cols = slice(g % 4 * 512, g % 4 * 512 + 512)
                        out = kt[:, 0, EDGE + cols.start:EDGE + cols.stop] if g < 4 else qs[:, cols]
                        nc.scalar.copy(out, scores[:, g % 4].rearrange("p s k -> p (s k)")).then_inc(S["prep_hi"], 1)

                def exp(n, w):
                    act.wait_ge(S["negmax"], n + (w + 1 + START))
                    act.wait_ge(S["e_turn"], n + (w - 3 + START))
                    p = pattern(w)
                    for s in range(2):
                        t = w % PAIRS * 2 + s
                        nc.scalar.activation(used(w, e[:, w % 4])[:, s], used(w, masked[:, w % 4])[:, s], ACT.Exp,
                                             bias=neg_max[:, w % 4, s:s + 1], scale=SCALE,
                                             accum_out=md_head[:, p, t, 1:2]).then_inc(S["exp"], 1)

                def e_hi(n, w):
                    act.wait_ge(S["e_turn"], n + (w + 1 + START))
                    act.wait_ge(S["pv"], n + (w - 1 + START))
                    c = 4 if pattern(w) < 2 else 2
                    nc.scalar.copy(et_hi[:, w % 2, :c], turned[:, w % 2, :c]).then_inc(S["e_hi"], 1)

                def step(h, n, w):
                    if w == 0:
                        act.wait_ge(S["md"], h + START)
                    if now(w, EXP):
                        exp(n, w - EXP)
                    if now(w, TURN):
                        e_hi(n, w - TURN)

                for name in "prep_hi exp e_hi".split():
                    act.sem_inc(S[name], START)
                heads(act, prepare, step)

            @block.vector
            def _(dve):
                def prepare(h):
                    for g in range(8):
                        dve.wait_ge(S["prep_hi"], h * 8 + (g + 1 + START))
                        cols = slice(g % 4 * 512, g % 4 * 512 + 512)
                        src = scores[:, g % 4].rearrange("p s k -> p (s k)")
                        if g < 4:
                            edge = slice(EDGE + cols.start, EDGE + cols.stop)
                            nc.vector.tensor_tensor(kt[:, 1, edge], src, kt[:, 0, edge].bitcast(F32),
                                                    ALU.subtract).then_inc(S["prep_lo"], 1)
                        else:
                            nc.vector.tensor_tensor(qs[HD:, cols], src[HD:], qs[HD:, cols].bitcast(F32),
                                                    ALU.subtract).then_inc(S["prep_lo"], 1)
                    dve.wait_ge(S["md"], h + START)

                def mask(n, w):
                    dve.wait_ge(S["scored"], n + (w + 1 + START))
                    dve.wait_ge(S["exp"], n * 2 + (2 * w - 6 + START))
                    dve.sem_inc(masks_begun, 1)
                    p = pattern(w)
                    for s in range(2):
                        j, t = tile_of(w, s)[1], w % PAIRS * 2 + s
                        if SUB[p] == 1:
                            allowed, found = masks[:, 3, RADIUS:RADIUS + P], scores[:, w % 4, s, s * P:s * P + P]
                        else:
                            allowed = masks[:, 0 if j == 0 else 2 if j == SUB[p] - 1 else 1]
                            found = scores[:, w % 4, s]
                        nc.vector.tensor_tensor_reduce(used(w, masked[:, w % 4])[:, s], found, allowed, 1.0, -3e38,
                                                       ALU.add, ALU.max, md_head[:, p, t, 0:1]).then_inc(S["masked"], 1)
                    dve.wait_ge(S["masked"], n * 2 + (2 * w + 2 + START))
                    t = w % PAIRS * 2
                    nc.vector.tensor_scalar(neg_max[:, w % 4], md_head[:, p, t:t + 2, 0], -SCALE, None,
                                            ALU.mult).then_inc(S["negmax"], 1)

                def e_lo(n, w):
                    dve.wait_ge(S["e_hi"], n + (w + 1 + START))
                    c = 4 if pattern(w) < 2 else 2
                    nc.vector.tensor_tensor(et_lo[:, w % 2, :c], turned[:, w % 2, :c], et_hi[:, w % 2, :c].bitcast(F32),
                                            ALU.subtract).then_inc(S["e_lo"], 1)

                def output(h, n, w):
                    p = pattern(w)
                    dve.wait_ge(S["pv"], n + (w + 1 + START))
                    if w % PAIRS == 0:
                        dve.wait_ge(stored[p], h * STORES[p] + STORES[p])
                    t = w % PAIRS * 2
                    nc.vector.tensor_reduce(nout[:, p, t:t + 2], pv[:, w % 2, :, :2 * HD].rearrange(
                        "p s (u d) -> p s d u", u=2), AX.X, ALU.add).then_inc(S["out"], 1)

                def step(h, n, w):
                    if now(w, MASK):
                        mask(n, w - MASK)
                    if now(w, OUT):
                        output(h, n, w - OUT)
                    if now(w, TURN):
                        e_lo(n, w - TURN)
                    if w == WORK + LAST - 1:
                        dve.wait_ge(S["exp"], n * 2 + (2 * WORK + START))
                        nc.vector.tensor_copy(md_all[:, :, :, bass.ts(h, 1)].rearrange("p k t h c -> p (k t) (h c)"),
                                              md_head[:].rearrange("p k t c -> p (k t) c")).then_inc(S["md"], 1)

                for name in "prep_lo masked negmax e_lo out md".split():
                    dve.sem_inc(S[name], START)
                dve.wait_ge(const_in, 32)
                heads(dve, prepare, step)

            @block.gpsimd
            def _(pool):
                def zero(k, t):
                    if k:
                        pool.wait_ge(zeroed, k)
                    nc.gpsimd.memset(t.bitcast(F32), 0.0).then_inc(zeroed, 1)

                zero(0, kt[:, :, :EDGE])
                zero(1, kt[:, :, EDGE + SEQ:])
                for p in range(2):
                    d, b = PATTERNS[p][1], BASE[p]
                    v = v_hl[:, b:b + CHUNKS[p] * d].rearrange("p (r c) x -> p r c x", r=d)
                    zero(2 + 2 * p, v[:RADIUS, :, 0])
                    zero(3 + 2 * p, v[RADIUS:, :, SUB[p]])

            @block.tensor
            def _(pe):
                def prepare(h):
                    pe.wait_ge(raw_in, h * 32 + 32)
                    for g in range(8):
                        if g < 4:
                            pe.wait_ge(S["masked"], h * (WORK * 2) + START)
                        else:
                            pe.wait_ge(S["prep_lo"], h * 8 + (g - 3 + START))
                        for c in range(4):
                            ins = nc.tensor.transpose(scores[:, g % 4, c // 2, c % 2 * P:c % 2 * P + P],
                                                      raw[:, g // 4, g % 4 * 4 + c], ident[:])
                        ins.then_inc(S["prep_turn"], 1)
                    pe.wait_ge(S["prep_lo"], h * 8 + (8 + START))

                def score(n, w):
                    if w >= 4:
                        pe.wait_ge(S["masked"], n * 2 + (2 * w - 6 + START))
                    p = pattern(w)
                    d = PATTERNS[p][1]
                    for s in range(2):
                        r, j = tile_of(w, s)
                        first = j * P * d + r
                        queries = qs[:, first:first + (P - 1) * d + 1:d]
                        out = scores[:, w % 4, s]
                        for u in range(2):
                            if SUB[p] == 1:
                                r0 = r - s
                                keys = kt[:, u, EDGE:EDGE + SEQ].rearrange("p (k r) -> p r k", r=d)[:, r0:r0 + 2]
                                dst = out.rearrange("p (r k) -> p r k", r=2)
                            else:
                                start = EDGE + first - RADIUS * d
                                keys, dst = kt[:, u, start:start + (KEYS - 1) * d + 1:d], out
                            ins = nc.tensor.matmul(dst, queries, keys, start=(u == 0), stop=(u == 1))
                    ins.then_inc(S["scored"], 1)

                def turn(n, w):
                    pe.wait_ge(S["exp"], n * 2 + (2 * w + 2 + START))
                    pe.wait_ge(S["e_lo"], n + (w - 1 + START))
                    for s in range(2):
                        chunks = 2 if pattern(w) < 2 else 1
                        for c in range(chunks):
                            ins = nc.tensor.transpose(turned[:, w % 2, s * chunks + c],
                                                      e[:, w % 4, s, c * P:(c + 1) * P], ident[:])
                    ins.then_inc(S["e_turn"], 1)

                def values(h, n, w):
                    p = pattern(w)
                    if w % PAIRS == 0:
                        pe.wait_ge(v_in[p], h * V_LOADS[p] + V_LOADS[p])
                    pe.wait_ge(S["e_lo"], n + (w + 1 + START))
                    pe.wait_ge(S["out"], n + (w - 1 + START))
                    chunks = 2 if p < 2 else 1
                    for s in range(2):
                        r, j = tile_of(w, s)
                        for c in range(chunks):
                            v = v_hl[:, BASE[p] + r * CHUNKS[p] + j + c].unsqueeze(1).to_broadcast([P, 2, 2 * HD])
                            dst = pv[:, w % 2, s].rearrange("p (u x) -> p u x", u=2)
                            nc.tensor.matmul(dst, et_hi[:, w % 2, s * chunks + c], v, start=(c == 0), stop=False)
                            ins = nc.tensor.matmul(dst, et_lo[:, w % 2, s * chunks + c], v,
                                                   start=False, stop=(c == chunks - 1))
                    ins.then_inc(S["pv"], 1)

                def step(h, n, w):
                    if now(w, TURN):
                        turn(n, w - TURN)
                    if now(w, 0):
                        score(n, w)
                    if now(w, VALUES):
                        values(h, n, w - VALUES)

                for name in "prep_turn scored e_turn pv".split():
                    pe.sem_inc(S[name], START)
                pe.wait_ge(const_in, 32)
                pe.wait_ge(zeroed, 6)
                heads(pe, prepare, step)


def one_pass(eng, pair):
    with eng.Fori(0, PAIRS - 1) as i:
        pair(i, False)
    pair(PAIRS - 1, True)


def lagged_pass(eng, step, end):
    step(Tile(0, 0, 0), True, 2)
    with eng.Fori(0, PAIRS - 2) as i:
        step(Tile(i, i, 1), False, 2)
        step(Tile(i + 1, i + 1, 0), False, 2)
    for t in range(TILES - 3, TILES):
        step(Tile(t // 2, t // 2, t % 2), False, min(2, TILES - 1 - t))
    end(Tile(PAIRS - 1, PAIRS - 1, 1))


def mix_phase(kit):
    nc, D = kit.nc, kit.dram
    G, NP, H = 2, len(PATTERNS), MAPS
    with ExitStack() as mem:
        sb = lambda name, shape, dt=F32: mem.enter_context(nc.sbuf_tensor("d_" + name, shape, dt))
        ps = lambda name, shape: mem.enter_context(nc.psum_tensor("d_" + name, shape, F32))
        w_raw = sb("w_raw", [P, KC, GROUP])
        w_hi = sb("w_hi", [P, G, KC, GROUP], F32R)
        w_lo = sb("w_lo", [P, G, KC, GROUP], F32R)
        ident = sb("ident", [P, P])
        gain = sb("gain", [P, DM])
        half = sb("half", [P, 1])
        x = sb("x", [P, 2, DM])
        mixed = sb("mixed", [P, 2, DM])
        nd = sb("nd", [P, 2, NP * H, HD])
        md = sb("md", [P, 2, NP, H, 2])
        top = sb("top", [P, H])
        below = sb("below", [P, NP, H])
        weight = sb("weight", [P, NP, H])
        wden = sb("wden", [P, NP, H])
        total = sb("total", [P, H])
        rtotal = sb("rtotal", [P, H])
        share = sb("share", [P, NP, H])
        parts = sb("parts", [P, NP, H * HD])
        two = sb("two", [P, H * HD])
        mt_hi = sb("mt_hi", [P, 2, KC, P], F32R)
        mt_lo = sb("mt_lo", [P, 2, KC, P], F32R)
        h = sb("h", [P, 2, DM])
        junk = sb("junk", [P, DM])
        ssq, mean, rstd = (sb(s, [P, 2]) for s in ("ssq", "mean", "rstd"))
        hn = sb("hn", [P, 2, DM])
        xt = sb("xt", [P, 2, KC, P])
        m_turned = ps("m_turned", [P, 2, 4 * P])
        h_turned = ps("h_turned", [P, 2, 4 * P])
        acc = ps("acc", [P, 2, G, GROUP])

        const_in, w_in, half_set = kit.sem("d_const_in"), kit.sem("d_w_in"), kit.sem("d_half_set")
        x_in, nd_in, h_stored, xt_stored = (kit.sem_pair("d_" + s) for s in ("x_in", "nd_in", "h_stored", "xt_stored"))
        od_in = kit.sem_pair("d_od_in")
        names = ("w_hi w_lo top below weight wden total rtotal share parts two merged m_turn m_hi m_lo acc h ssq "
                 "mean rstd hn h_turn h_out")
        S = {name: kit.sem("d_" + name) for name in names.split()}

        with nc.Block() as block:

            @block.sync
            def _(sp):
                def load(a):
                    sp.wait_ge(S["h"], a.n * 2 - 2 + START)
                    sp.dma_start(x[:, a.s], D["x"][bass.ts(a.t, P)]).then_inc(x_in[a.s], 16)

                def load_attention(a):
                    sp.wait_ge(S["parts"], a.n - 1 + START)
                    sp.wait_ge(S["m_turn"], a.n * 2 - 2 + START)
                    for k in range(NP):
                        sp.dma_start(nd[:, a.s, k * H:(k + 1) * H], D["nd"][k, bass.ts(a.t, P)]).then_inc(nd_in[a.s], 16)
                    sp.dma_start(md[:, a.s].rearrange("p k h c -> p k (h c)"), D["md"][:, bass.ts(a.t, P)].rearrange(
                        "k p h c -> p k (h c)")).then_inc(nd_in[a.s], 16)
                    sp.dma_start(mixed[:, a.s, :GROUP], D["od"][bass.ts(a.t, P)]).then_inc(od_in[a.s], 16)

                def store(a):
                    sp.wait_ge(S["h"], a.n * 2 + (2 + START))
                    sp.dma_start(D["h"][bass.ts(a.t, P)], h[:, a.s]).then_inc(h_stored[a.s], 16)

                def store_turned(a):
                    sp.wait_ge(S["h_out"], a.n * 2 + (2 + START))
                    sp.dma_start(D["xt"][a.t], xt[:, a.s]).then_inc(xt_stored[a.s], 16)

                for s in range(2):
                    sp.sem_inc(h_stored[s], 16)
                    sp.sem_inc(xt_stored[s], 16)
                load_attention(Tile(0, 0, 0))
                sp.dma_start(ident[:], D["ident"][:]).then_inc(const_in, 16)
                sp.dma_start(gain[:], D["g_mlp"].partition_broadcast(P)).then_inc(const_in, 16)
                for g in range(G):
                    sp.wait_ge(S["w_lo"], g + START)
                    sp.dma_start(w_raw[:], D["w_out"][:, g * GROUP:(g + 1) * GROUP].rearrange(
                        "(c p) n -> p c n", p=P)).then_inc(w_in, 16)
                    if g == 0:
                        load_attention(Tile(0, 0, 1))
                        load(Tile(0, 0, 0))
                        load(Tile(0, 0, 1))

                def step(a, first, more):
                    if more == 2:
                        load_attention(a.next(2))
                    store(a)
                    if more == 2:
                        load(a.next(2))
                    if not first:
                        store_turned(a.before())

                lagged_pass(sp, step, store_turned)
                for s in range(2):
                    sp.wait_ge(h_stored[s], 16 * (PAIRS + 1))
                    sp.wait_ge(xt_stored[s], 16 * (PAIRS + 1))

            @block.scalar
            def _(act):
                def split_w(g):
                    act.wait_ge(w_in, 16 * (g + 1))
                    nc.scalar.copy(w_hi[:, g], w_raw[:]).then_inc(S["w_hi"], 1)

                def weigh(a):
                    act.wait_ge(S["below"], a.n + (1 + START))
                    act.wait_ge(S["share"], a.n + START)
                    nc.scalar.activation(weight[:], below[:], ACT.Exp, scale=SCALE).then_inc(S["weight"], 1)

                def m_hi(a):
                    act.wait_ge(S["acc"], a.n * 2 - 2 + START)
                    for b in range(2):
                        act.wait_ge(S["m_turn"], a.n * 2 + (b + 1 + START))
                        nc.scalar.copy(mt_hi[:, a.s, 4 * b:4 * b + 4].rearrange("p c t -> p (c t)"),
                                       m_turned[:, b]).then_inc(S["m_hi"], 1)

                def square(a):
                    act.wait_ge(S["h"], a.n * 2 + (2 + START))
                    act.wait_ge(S["ssq"], a.n + START)
                    nc.scalar.activation(junk[:], h[:, a.s], ACT.Square,
                                         accum_out=ssq[:, a.s:a.s + 1]).then_inc(S["ssq"], 1)

                def h_out(a):
                    act.wait_ge(xt_stored[a.s], a.j * 16 + 16)
                    for b in range(2):
                        act.wait_ge(S["h_turn"], a.n * 2 + (b + 1 + START))
                        nc.scalar.copy(xt[:, a.s, 4 * b:4 * b + 4].rearrange("p c t -> p (c t)"),
                                       h_turned[:, b]).then_inc(S["h_out"], 1)

                for name in "w_hi weight m_hi ssq h_out".split():
                    act.sem_inc(S[name], START)
                weigh(Tile(0, 0, 0))
                split_w(0)
                m_hi(Tile(0, 0, 0))
                split_w(1)
                weigh(Tile(0, 0, 1))

                def step(a, first, more):
                    if more:
                        m_hi(a.next(1))
                    if more == 2:
                        weigh(a.next(2))
                    square(a)
                    if not first:
                        h_out(a.before())

                lagged_pass(act, step, h_out)

            @block.vector
            def _(dve):
                def split_w(g):
                    dve.wait_ge(S["w_hi"], g + 1 + START)
                    nc.vector.tensor_tensor(w_lo[:, g], w_raw[:], w_hi[:, g].bitcast(F32),
                                            ALU.subtract).then_inc(S["w_lo"], 1)

                def maxima(a):
                    dve.wait_ge(nd_in[a.s], a.j * 64 + 64)
                    dve.wait_ge(S["below"], a.n + START)
                    nc.vector.tensor_reduce(top[:], md[:, a.s, :, :, 0].rearrange("p k h -> p h k"),
                                            AX.X, ALU.max).then_inc(S["top"], 1)
                    dve.wait_ge(S["top"], a.n + (1 + START))
                    dve.wait_ge(S["weight"], a.n + START)
                    nc.vector.tensor_tensor(below[:], md[:, a.s, :, :, 0], top[:].unsqueeze(1).to_broadcast([P, NP, H]),
                                            ALU.subtract).then_inc(S["below"], 1)

                def merge(a):
                    dve.wait_ge(S["weight"], a.n + (1 + START))
                    nc.vector.tensor_tensor(wden[:], weight[:], md[:, a.s, :, :, 1], ALU.mult).then_inc(S["wden"], 1)
                    dve.wait_ge(S["wden"], a.n + (1 + START))
                    nc.vector.tensor_reduce(total[:], wden[:].rearrange("p k h -> p h k"),
                                            AX.X, ALU.add).then_inc(S["total"], 1)
                    dve.wait_ge(S["total"], a.n + (1 + START))
                    nc.vector.reciprocal(rtotal[:], total[:]).then_inc(S["rtotal"], 1)
                    dve.wait_ge(S["rtotal"], a.n + (1 + START))
                    nc.vector.tensor_tensor(share[:], weight[:], rtotal[:].unsqueeze(1).to_broadcast([P, NP, H]),
                                            ALU.mult).then_inc(S["share"], 1)
                    dve.wait_ge(S["share"], a.n + (1 + START))
                    dve.wait_ge(S["merged"], a.n + START)
                    nc.vector.tensor_tensor(
                        parts[:].rearrange("p k (h d) -> p (k h) d", d=HD), nd[:, a.s],
                        share[:].rearrange("p k h -> p (k h)").unsqueeze(2).to_broadcast([P, NP * H, HD]),
                        ALU.mult).then_inc(S["parts"], 1)

                def lo(a, bank, hi, out, done_hi, done):
                    for b in range(2):
                        dve.wait_ge(S[done_hi], a.n * 2 + (b + 1 + START))
                        view = lambda t: t[:, a.s, 4 * b:4 * b + 4].rearrange("p c t -> p (c t)")
                        nc.vector.tensor_tensor(view(out), bank[:, b], view(hi).bitcast(F32),
                                                ALU.subtract).then_inc(S[done], 1)

                def residual(a):
                    dve.wait_ge(x_in[a.s], a.j * 16 + 16)
                    dve.wait_ge(h_stored[a.s], a.j * 16 + 16)
                    for g in range(G):
                        dve.wait_ge(S["acc"], a.n * 2 + (g + 1 + START))
                        cols = slice(g * GROUP, (g + 1) * GROUP)
                        nc.vector.tensor_tensor(h[:, a.s, cols], acc[:, a.s, g], x[:, a.s, cols],
                                                ALU.add).then_inc(S["h"], 1)

                def normalise(a):
                    v = slice(a.s, a.s + 1)
                    dve.wait_ge(S["ssq"], a.n + (1 + START))
                    nc.vector.tensor_scalar(mean[:, v], ssq[:, v], 1.0 / DM, NORM_EPS,
                                            ALU.mult, ALU.add).then_inc(S["mean"], 1)
                    dve.wait_ge(S["rstd"], a.n + (1 + START))
                    dve.wait_ge(S["h_turn"], a.n * 2 - 2 + START)
                    nc.vector.scalar_tensor_tensor(out=hn[:, a.s], in0=h[:, a.s], scalar=rstd[:, v], in1=gain[:],
                                                   op0=ALU.mult, op1=ALU.mult).then_inc(S["hn"], 1)

                for name in "w_lo top below wden total rtotal share parts m_lo h mean hn".split():
                    dve.sem_inc(S[name], START)
                dve.wait_ge(const_in, 32)
                maxima(Tile(0, 0, 0))
                merge(Tile(0, 0, 0))
                split_w(0)
                lo(Tile(0, 0, 0), m_turned, mt_hi, mt_lo, "m_hi", "m_lo")
                split_w(1)
                maxima(Tile(0, 0, 1))
                merge(Tile(0, 0, 1))

                def step(a, first, more):
                    if more:
                        lo(a.next(1), m_turned, mt_hi, mt_lo, "m_hi", "m_lo")
                    if more == 2:
                        maxima(a.next(2))
                        merge(a.next(2))
                    residual(a)
                    normalise(a)

                lagged_pass(dve, step, lambda a: None)

            @block.gpsimd
            def _(pool):
                def merge(a):
                    pool.wait_ge(S["parts"], a.n + (1 + START))
                    nc.gpsimd.tensor_tensor(two[:], parts[:, 0], parts[:, 1], ALU.add).then_inc(S["two"], 1)
                    pool.wait_ge(S["two"], a.n + (1 + START))
                    pool.wait_ge(S["m_turn"], a.n * 2 - 2 + START)
                    nc.gpsimd.tensor_tensor(mixed[:, a.s, GROUP:], two[:], parts[:, 2], ALU.add).then_inc(S["merged"], 1)

                def root(a):
                    v = slice(a.s, a.s + 1)
                    pool.wait_ge(S["mean"], a.n + (1 + START))
                    nc.gpsimd.tensor_tensor(rstd[:, v], mean[:, v], half[:], ALU.pow).then_inc(S["rstd"], 1)

                for name in "two merged rstd".split():
                    pool.sem_inc(S[name], START)
                nc.gpsimd.memset(half[:], -0.5).then_inc(half_set, 1)
                pool.wait_ge(half_set, 1)
                merge(Tile(0, 0, 0))
                merge(Tile(0, 0, 1))

                def step(a, first, more):
                    if more == 2:
                        merge(a.next(2))
                    root(a)

                lagged_pass(pool, step, lambda a: None)

            @block.tensor
            def _(pe):
                def turn(a, bank, src, before, done, gate):
                    gate(a)
                    for b in range(2):
                        pe.wait_ge(S[before], a.n * 2 + (b - 1 + START))
                        for c in range(4):
                            ins = nc.tensor.transpose(bank[:, b, c * P:(c + 1) * P],
                                                      src[:, a.s, (4 * b + c) * P:(4 * b + c + 1) * P], ident[:])
                        ins.then_inc(S[done], 1)

                def mixed_ready(a):
                    pe.wait_ge(S["merged"], a.n + (1 + START))
                    pe.wait_ge(od_in[a.s], a.j * 16 + 16)

                def hn_ready(a):
                    pe.wait_ge(S["hn"], a.n + (1 + START))

                def project(a):
                    pe.wait_ge(S["m_lo"], a.n * 2 + (2 + START))
                    for g in range(G):
                        pe.wait_ge(S["w_lo"], g + 1 + START)
                        pe.wait_ge(S["h"], a.n * 2 + (g - 3 + START))
                        for c in range(KC):
                            ins = matmul3(nc, acc[:, a.s, g], mt_hi[:, a.s, c], mt_lo[:, a.s, c],
                                          w_hi[:, g, c], w_lo[:, g, c], c == 0, c == KC - 1)
                        ins.then_inc(S["acc"], 1)

                for name in "m_turn acc h_turn".split():
                    pe.sem_inc(S[name], START)
                pe.wait_ge(const_in, 32)
                turn(Tile(0, 0, 0), m_turned, mixed, "m_lo", "m_turn", mixed_ready)

                def turn_h(a):
                    turn(a, h_turned, hn, "h_out", "h_turn", hn_ready)

                def step(a, first, more):
                    if more:
                        turn(a.next(1), m_turned, mixed, "m_lo", "m_turn", mixed_ready)
                    project(a)
                    if not first:
                        turn_h(a.before())

                lagged_pass(pe, step, turn_h)


def mlp_phase(kit):
    nc, D = kit.nc, kit.dram
    FB, FT, TB = D_FF // 256, 2, 2
    HALVES, HT = 2, TILES // 2
    H_SLOTS = HT + 5
    with ExitStack() as mem:
        sb = lambda name, shape, dt=F32: mem.enter_context(nc.sbuf_tensor("e_" + name, shape, dt))
        ps = lambda name, shape: mem.enter_context(nc.psum_tensor("e_" + name, shape, F32))
        xt_hi = sb("xt_hi", [P, KC, HT * P], F32R)
        xt_lo = sb("xt_lo", [P, KC, HT * P], F32R)
        h = sb("h", [P, H_SLOTS, DM])
        up_raw = sb("up_raw", [P, KC, 256])
        up_hi, up_lo = sb("up_hi", [P, KC, 256], F32R), sb("up_lo", [P, KC, 256], F32R)
        down_raw = sb("down_raw", [P, FT, DM])
        down_hi, down_lo = sb("down_hi", [P, FT, DM], F32R), sb("down_lo", [P, FT, DM], F32R)
        r = sb("r", [P, 2, 512])
        sq = sb("sq", [P, 2, 512])
        u_hi = sb("u_hi", [P, FT, HT * P], F32R)
        u_lo = sb("u_lo", [P, FT, HT * P], F32R)
        up_acc = ps("up_acc", [P, 2, 512])
        down_acc = ps("down_acc", [P, 4, 512])

        xt_in = [kit.sem(f"e_xt_in{t}") for t in range(HT)]
        h_in, stored = ([kit.sem(f"e_{s}{t}") for t in range(TILES)] for s in ("h_in", "stored"))
        up_in, down_in = kit.sem("e_up_in"), kit.sem("e_down_in")
        names = "xt_hi xt_lo up_hi up_lo down_hi down_lo up_acc relu sq u_hi u_lo down_acc h"
        S = {name: kit.sem("e_" + name) for name in names.split()}
        UNITS = [(f, t) for t in range(TB) for f in range(FT)]
        DU = HT * 2

        def slot(z, t):
            return (z * HT + t) % H_SLOTS

        def blocks(eng, step):
            for z in range(HALVES):
                step(z, 0, z * FB, 1)
                with eng.Fori(1, FB - 1) as f:
                    step(z, f, f + z * FB, f + 1)
                step(z, FB - 1, z * FB + FB - 1, None)

        with nc.Block() as block:

            @block.sync
            def _(sp):
                def load_xt(z, t):
                    if z:
                        sp.wait_ge(S["up_acc"], z * FB * 4 + START)
                    sp.dma_start(xt_lo[:, :, t * P:(t + 1) * P].bitcast(F32), D["xt"][z * HT + t]).then_inc(xt_in[t], 16)

                def load_h(z, t):
                    before = z * HT + t - H_SLOTS
                    if before >= 0:
                        sp.wait_ge(stored[before], 16)
                    sp.dma_start(h[:, slot(z, t)], D["h"][(z * HT + t) * P:(z * HT + t + 1) * P]
                                 ).then_inc(h_in[z * HT + t], 16)

                def load_weights(f, n):
                    sp.wait_ge(S["up_lo"], n + START)
                    sp.dma_start(up_raw[:], D["w_up"].rearrange("(c p) (f n) -> f p c n", p=P, n=256)[f]
                                 ).then_inc(up_in, 16)
                    sp.wait_ge(S["down_lo"], n + START)
                    sp.dma_start(down_raw[:], D["w_down"].rearrange("(f c p) d -> f p c d", p=P, c=FT)[f]
                                 ).then_inc(down_in, 16)

                def step(z, f, n, following):
                    if following is not None:
                        load_weights(following, n + 1)
                        return
                    if z + 1 < HALVES:
                        load_weights(0, n + 1)
                        for t in range(HT):
                            load_xt(z + 1, t)
                    for t in range(HT):
                        sp.wait_ge(S["h"], n * DU + (2 * t + 2 + START))
                        sp.dma_start(D["h2"][(z * HT + t) * P:(z * HT + t + 1) * P], h[:, slot(z, t)]
                                     ).then_inc(stored[z * HT + t], 16)
                    if z + 1 < HALVES:
                        for t in range(H_SLOTS - HT, HT):
                            load_h(z + 1, t)

                load_xt(0, 0)
                sp.dma_start(up_raw[:], D["w_up"].rearrange("(c p) (f n) -> f p c n", p=P, n=256)[0]).then_inc(up_in, 16)
                for t in range(1, HT // TB):
                    load_xt(0, t)
                sp.dma_start(down_raw[:], D["w_down"].rearrange("(f c p) d -> f p c d", p=P, c=FT)[0]).then_inc(down_in, 16)
                for t in range(HT // TB, HT):
                    load_xt(0, t)
                for t in range(HT):
                    load_h(0, t)
                for t in range(H_SLOTS - HT):
                    load_h(1, t)
                blocks(sp, step)
                for t in range(TILES):
                    sp.wait_ge(stored[t], 16)

            @block.scalar
            def _(act):
                def split_xt(z, tiles):
                    for t in tiles:
                        act.wait_ge(xt_in[t], z * 16 + 16)
                        nc.scalar.copy(xt_hi[:, :, t * P:(t + 1) * P],
                                       xt_lo[:, :, t * P:(t + 1) * P].bitcast(F32)).then_inc(S["xt_hi"], 1)

                def split_up(n):
                    act.wait_ge(up_in, n * 16 + 16)
                    act.wait_ge(S["up_acc"], n * 4 + START)
                    nc.scalar.copy(up_hi[:], up_raw[:]).then_inc(S["up_hi"], 1)

                def step(z, f, n, following):
                    act.wait_ge(down_in, n * 16 + 16)
                    act.wait_ge(S["down_acc"], n * DU + START)
                    nc.scalar.copy(down_hi[:], down_raw[:]).then_inc(S["down_hi"], 1)
                    if isinstance(f, int) and f == 0:
                        split_xt(z, range(HT // TB, HT))
                    for k, (ft, tb) in enumerate(UNITS):
                        act.wait_ge(S["up_acc"], n * 4 + (k + 1 + START))
                        act.wait_ge(S["sq"], n * 4 + (k - 1 + START))
                        nc.scalar.activation(r[:, k % 2], up_acc[:, k % 2], ACT.Relu).then_inc(S["relu"], 1)
                        act.wait_ge(S["sq"], n * 4 + (k + 1 + START))
                        nc.scalar.copy(u_hi[:, ft, tb * 512:(tb + 1) * 512], sq[:, k % 2]).then_inc(S["u_hi"], 1)
                    if following is not None or z + 1 < HALVES:
                        split_up(n + 1)
                    if following is None and z + 1 < HALVES:
                        split_xt(z + 1, range(HT // TB))

                for name in "xt_hi up_hi down_hi relu u_hi".split():
                    act.sem_inc(S[name], START)
                split_xt(0, range(1))
                split_up(0)
                split_xt(0, range(1, HT // TB))
                blocks(act, step)

            @block.vector
            def _(dve):
                def split_xt(z, tiles):
                    for t in tiles:
                        dve.wait_ge(S["xt_hi"], z * HT + t + 1 + START)
                        tile = xt_lo[:, :, t * P:(t + 1) * P]
                        nc.vector.tensor_tensor(tile, tile.bitcast(F32), xt_hi[:, :, t * P:(t + 1) * P].bitcast(F32),
                                                ALU.subtract).then_inc(S["xt_lo"], 1)

                def split_up(n):
                    dve.wait_ge(S["up_hi"], n + (1 + START))
                    nc.vector.tensor_tensor(up_lo[:], up_raw[:], up_hi[:].bitcast(F32),
                                            ALU.subtract).then_inc(S["up_lo"], 1)

                def step(z, f, n, following):
                    dve.wait_ge(S["down_hi"], n + (1 + START))
                    nc.vector.tensor_tensor(down_lo[:], down_raw[:], down_hi[:].bitcast(F32),
                                            ALU.subtract).then_inc(S["down_lo"], 1)
                    first = isinstance(f, int) and f == 0
                    if first:
                        split_xt(z, range(HT // TB, HT))
                    for k in range(DU):
                        t, g = k // 2, k % 2
                        dve.wait_ge(S["down_acc"], n * DU + (k + 1 + START))
                        if first and g == 0:
                            dve.wait_ge(h_in[z * HT + t], 16)
                        if k == 0:
                            dve.wait_ge(S["h"], n * DU + START)
                        cols = slice(g * 512, (g + 1) * 512)
                        nc.vector.tensor_tensor(h[:, slot(z, t), cols], down_acc[:, k % 4], h[:, slot(z, t), cols],
                                                ALU.add).then_inc(S["h"], 1)
                        if k == 2 and (following is not None or z + 1 < HALVES):
                            split_up(n + 1)
                        if following is None and z + 1 < HALVES and k % 3 == 1 and k >= 4:
                            split_xt(z + 1, [(k - 4) // 3])

                for name in "xt_lo up_lo down_lo h".split():
                    dve.sem_inc(S[name], START)
                split_xt(0, range(1))
                split_up(0)
                split_xt(0, range(1, HT // TB))
                blocks(dve, step)

            @block.gpsimd
            def _(pool):
                def step(z, f, n, following):
                    for k, (ft, tb) in enumerate(UNITS):
                        pool.wait_ge(S["relu"], n * 4 + (k + 1 + START))
                        pool.wait_ge(S["u_lo"], n * 4 + (k - 1 + START))
                        nc.gpsimd.tensor_tensor(sq[:, k % 2], r[:, k % 2], r[:, k % 2], ALU.mult).then_inc(S["sq"], 1)
                        pool.wait_ge(S["u_hi"], n * 4 + (k + 1 + START))
                        cols = slice(tb * 512, (tb + 1) * 512)
                        nc.gpsimd.tensor_tensor(u_lo[:, ft, cols], sq[:, k % 2], u_hi[:, ft, cols].bitcast(F32),
                                                ALU.subtract).then_inc(S["u_lo"], 1)

                for name in "sq u_lo".split():
                    pool.sem_inc(S[name], START)
                blocks(pool, step)

            @block.tensor
            def _(pe):
                def step(z, f, n, following):
                    pe.wait_ge(S["up_lo"], n + (1 + START))
                    for k, (ft, tb) in enumerate(UNITS):
                        if isinstance(f, int) and f == 0:
                            if ft == 0:
                                pe.wait_ge(S["xt_lo"], z * HT + (tb + 1) * (HT // TB) + START)
                        pe.wait_ge(S["relu"], n * 4 + (k - 1 + START))
                        cols = slice(tb * 512, (tb + 1) * 512)
                        for c in range(KC):
                            ins = matmul3(nc, up_acc[:, k % 2], up_hi[:, c, ft * P:(ft + 1) * P],
                                          up_lo[:, c, ft * P:(ft + 1) * P], xt_hi[:, c, cols], xt_lo[:, c, cols],
                                          c == 0, c == KC - 1)
                        ins.then_inc(S["up_acc"], 1)
                    pe.wait_ge(S["down_lo"], n + (1 + START))
                    for k in range(DU):
                        t, g = k // 2, k % 2
                        if k % (DU // TB) == 0:
                            pe.wait_ge(S["u_lo"], n * 4 + ((k // (DU // TB) + 1) * FT + START))
                        pe.wait_ge(S["h"], n * DU + (k - 3 + START))
                        toks, cols = slice(t * P, (t + 1) * P), slice(g * 512, (g + 1) * 512)
                        for c in range(FT):
                            ins = matmul3(nc, down_acc[:, k % 4], u_hi[:, c, toks], u_lo[:, c, toks],
                                          down_hi[:, c, cols], down_lo[:, c, cols], c == 0, c == FT - 1)
                        ins.then_inc(S["down_acc"], 1)

                for name in "up_acc down_acc".split():
                    pe.sem_inc(S[name], START)
                blocks(pe, step)


def gate_phase(kit):
    nc, D = kit.nc, kit.dram
    G, PC = 2, D_PLE // P
    with ExitStack() as mem:
        sb = lambda name, shape, dt=F32: mem.enter_context(nc.sbuf_tensor("f_" + name, shape, dt))
        ps = lambda name, shape: mem.enter_context(nc.psum_tensor("f_" + name, shape, F32))
        w_raw = sb("w_raw", [P, KC, GROUP])
        w_hi, w_lo = sb("w_hi", [P, G, KC, GROUP], F32R), sb("w_lo", [P, G, KC, GROUP], F32R)
        e_raw = sb("e_raw", [P, PC, DM])
        e_hi, e_lo = sb("e_hi", [P, PC, DM], F32R), sb("e_lo", [P, PC, DM], F32R)
        ident = sb("ident", [P, P])
        gain, gain_final = sb("gain", [P, DM]), sb("gain_final", [P, DM])
        half = sb("half", [P, 1])
        h, hn = sb("h", [P, 2, DM]), sb("hn", [P, 2, DM])
        res = sb("res", [P, 2, DM])
        emb = sb("emb", [P, 2, D_PLE])
        junk, junk2 = sb("junk", [P, DM]), sb("junk2", [P, DM])
        ssq, mean, rstd = (sb(s, [P, 2]) for s in ("ssq", "mean", "rstd"))
        ssq2, mean2, rstd2 = (sb(s, [P, 2]) for s in ("ssq2", "mean2", "rstd2"))
        xt_hi, xt_lo = sb("xt_hi", [P, 2, KC, P], F32R), sb("xt_lo", [P, 2, KC, P], F32R)
        et_hi, et_lo = sb("et_hi", [P, 2, PC, P], F32R), sb("et_lo", [P, 2, PC, P], F32R)
        gate = sb("gate", [P, G, GROUP])
        gated = sb("gated", [P, G, GROUP])
        h3 = sb("h3", [P, 2, DM])
        out = sb("out", [P, 2, DM])
        turned = ps("turned", [P, 2, 4 * P])
        e_turned = ps("e_turned", [P, 4 * P])
        gate_acc, emb_acc = ps("gate_acc", [P, G, GROUP]), ps("emb_acc", [P, G, GROUP])

        const_in, w_in, e_in, half_set = (kit.sem("f_" + s) for s in ("const_in", "w_in", "e_in", "half_set"))
        h_in, res_in, emb_in, stored = (kit.sem_pair("f_" + s) for s in ("h_in", "res_in", "emb_in", "stored"))
        names = ("w_hi w_lo e_whi e_wlo ssq mean rstd hn turn hi lo e_turn e_hi e_lo gate_acc emb_acc gate gated h3 "
                 "ssq2 mean2 rstd2 out")
        S = {name: kit.sem("f_" + name) for name in names.split()}

        with nc.Block() as block:

            @block.sync
            def _(sp):
                def load(a):
                    sp.wait_ge(S["hn"], a.n - 1 + START)
                    sp.dma_start(h[:, a.s], D["h2"][bass.ts(a.t, P)]).then_inc(h_in[a.s], 16)
                    sp.wait_ge(S["e_turn"], a.n - 1 + START)
                    sp.dma_start(emb[:, a.s], D["p"][bass.ts(a.t, P)]).then_inc(emb_in[a.s], 16)

                def load_again(a):
                    sp.wait_ge(S["h3"], a.n * 2 - 2 + START)
                    sp.dma_start(res[:, a.s], D["h2"][bass.ts(a.t, P)]).then_inc(res_in[a.s], 16)

                def store(a):
                    sp.wait_ge(S["out"], a.n + (1 + START))
                    sp.dma_start(D["out"][bass.ts(a.t, P)], out[:, a.s]).then_inc(stored[a.s], 16)

                for s in range(2):
                    sp.sem_inc(stored[s], 16)
                load(Tile(0, 0, 0))
                sp.dma_start(ident[:], D["ident"][:]).then_inc(const_in, 16)
                sp.dma_start(gain[:], D["g_ple"].partition_broadcast(P)).then_inc(const_in, 16)
                sp.dma_start(gain_final[:], D["g_final"].partition_broadcast(P)).then_inc(const_in, 16)
                for g in range(G):
                    sp.wait_ge(S["w_lo"], g + START)
                    sp.dma_start(w_raw[:], D["w_ple_gate"][:, g * GROUP:(g + 1) * GROUP].rearrange(
                        "(c p) n -> p c n", p=P)).then_inc(w_in, 16)
                    if g == 0:
                        sp.dma_start(e_raw[:], D["w_ple_proj"].rearrange("(c p) n -> p c n", p=P)).then_inc(e_in, 16)
                        load(Tile(0, 0, 1))
                        load_again(Tile(0, 0, 0))

                def pair(j, last):
                    for s in range(2):
                        a = Tile(j, j, s)
                        if not last:
                            load(a.next(2))
                        if not (last and s == 1):
                            load_again(a.next(1))
                        store(a)

                one_pass(sp, pair)
                for s in range(2):
                    sp.wait_ge(stored[s], 16 * (PAIRS + 1))

            @block.scalar
            def _(act):
                def split_w(g):
                    act.wait_ge(w_in, 16 * (g + 1))
                    nc.scalar.copy(w_hi[:, g], w_raw[:]).then_inc(S["w_hi"], 1)

                def square(a):
                    act.wait_ge(h_in[a.s], a.j * 16 + 16)
                    act.wait_ge(S["ssq"], a.n + START)
                    nc.scalar.activation(junk[:], h[:, a.s], ACT.Square,
                                         accum_out=ssq[:, a.s:a.s + 1]).then_inc(S["ssq"], 1)

                def hi(a):
                    act.wait_ge(S["emb_acc"], a.n * 2 - 2 + START)
                    for b in range(2):
                        act.wait_ge(S["turn"], a.n * 2 + (b + 1 + START))
                        nc.scalar.copy(xt_hi[:, a.s, 4 * b:4 * b + 4].rearrange("p c t -> p (c t)"),
                                       turned[:, b]).then_inc(S["hi"], 1)
                    act.wait_ge(S["e_turn"], a.n + (1 + START))
                    nc.scalar.copy(et_hi[:, a.s].rearrange("p c t -> p (c t)"), e_turned[:, :PC * P]).then_inc(S["e_hi"], 1)

                def sigmoid(a):
                    for g in range(G):
                        act.wait_ge(S["gate_acc"], a.n * 2 + (g + 1 + START))
                        act.wait_ge(S["gated"], a.n * 2 + (g - 1 + START))
                        nc.scalar.activation(gate[:, g], gate_acc[:, g], ACT.Sigmoid).then_inc(S["gate"], 1)

                def square2(a):
                    act.wait_ge(S["h3"], a.n * 2 + (2 + START))
                    act.wait_ge(S["ssq2"], a.n + START)
                    nc.scalar.activation(junk2[:], h3[:, a.s], ACT.Square,
                                         accum_out=ssq2[:, a.s:a.s + 1]).then_inc(S["ssq2"], 1)

                for name in "w_hi e_whi ssq hi e_hi gate ssq2".split():
                    act.sem_inc(S[name], START)
                square(Tile(0, 0, 0))
                split_w(0)
                hi(Tile(0, 0, 0))
                act.wait_ge(e_in, 16)
                nc.scalar.copy(e_hi[:], e_raw[:]).then_inc(S["e_whi"], 1)
                split_w(1)
                square(Tile(0, 0, 1))

                def pair(j, last):
                    for s in range(2):
                        a = Tile(j, j, s)
                        if not (last and s == 1):
                            hi(a.next(1))
                        if not last:
                            square(a.next(2))
                        sigmoid(a)
                        square2(a)

                one_pass(act, pair)

            @block.vector
            def _(dve):
                def split_w(g):
                    dve.wait_ge(S["w_hi"], g + 1 + START)
                    nc.vector.tensor_tensor(w_lo[:, g], w_raw[:], w_hi[:, g].bitcast(F32),
                                            ALU.subtract).then_inc(S["w_lo"], 1)

                def normalise(a):
                    v = slice(a.s, a.s + 1)
                    dve.wait_ge(S["ssq"], a.n + (1 + START))
                    nc.vector.tensor_scalar(mean[:, v], ssq[:, v], 1.0 / DM, NORM_EPS,
                                            ALU.mult, ALU.add).then_inc(S["mean"], 1)
                    dve.wait_ge(S["rstd"], a.n + (1 + START))
                    dve.wait_ge(S["turn"], a.n * 2 - 2 + START)
                    nc.vector.scalar_tensor_tensor(out=hn[:, a.s], in0=h[:, a.s], scalar=rstd[:, v], in1=gain[:],
                                                   op0=ALU.mult, op1=ALU.mult).then_inc(S["hn"], 1)

                def lo(a):
                    for b in range(2):
                        dve.wait_ge(S["hi"], a.n * 2 + (b + 1 + START))
                        view = lambda t: t[:, a.s, 4 * b:4 * b + 4].rearrange("p c t -> p (c t)")
                        nc.vector.tensor_tensor(view(xt_lo), turned[:, b], view(xt_hi).bitcast(F32),
                                                ALU.subtract).then_inc(S["lo"], 1)
                    dve.wait_ge(S["e_hi"], a.n + (1 + START))
                    view = lambda t: t[:, a.s].rearrange("p c t -> p (c t)")
                    nc.vector.tensor_tensor(view(et_lo), e_turned[:, :PC * P], view(et_hi).bitcast(F32),
                                            ALU.subtract).then_inc(S["e_lo"], 1)

                def gate_in(a):
                    for g in range(G):
                        dve.wait_ge(S["gate"], a.n * 2 + (g + 1 + START))
                        dve.wait_ge(S["emb_acc"], a.n * 2 + (g + 1 + START))
                        dve.wait_ge(S["h3"], a.n * 2 + (g - 1 + START))
                        nc.vector.tensor_tensor(gated[:, g], emb_acc[:, g], gate[:, g], ALU.mult).then_inc(S["gated"], 1)

                def finish(a):
                    v = slice(a.s, a.s + 1)
                    dve.wait_ge(S["ssq2"], a.n + (1 + START))
                    nc.vector.tensor_scalar(mean2[:, v], ssq2[:, v], 1.0 / DM, NORM_EPS,
                                            ALU.mult, ALU.add).then_inc(S["mean2"], 1)
                    dve.wait_ge(S["rstd2"], a.n + (1 + START))
                    dve.wait_ge(stored[a.s], a.j * 16 + 16)
                    nc.vector.scalar_tensor_tensor(out=out[:, a.s], in0=h3[:, a.s], scalar=rstd2[:, v],
                                                   in1=gain_final[:], op0=ALU.mult, op1=ALU.mult).then_inc(S["out"], 1)

                for name in "w_lo e_wlo mean hn lo e_lo gated mean2 out".split():
                    dve.sem_inc(S[name], START)
                dve.wait_ge(const_in, 48)
                normalise(Tile(0, 0, 0))
                split_w(0)
                lo(Tile(0, 0, 0))
                dve.wait_ge(S["e_whi"], 1 + START)
                nc.vector.tensor_tensor(e_lo[:], e_raw[:], e_hi[:].bitcast(F32), ALU.subtract).then_inc(S["e_wlo"], 1)
                split_w(1)
                normalise(Tile(0, 0, 1))

                def pair(j, last):
                    for s in range(2):
                        a = Tile(j, j, s)
                        if not (last and s == 1):
                            lo(a.next(1))
                        if not last:
                            normalise(a.next(2))
                        gate_in(a)
                        finish(a)

                one_pass(dve, pair)

            @block.gpsimd
            def _(pool):
                def root(a):
                    v = slice(a.s, a.s + 1)
                    pool.wait_ge(S["mean"], a.n + (1 + START))
                    nc.gpsimd.tensor_tensor(rstd[:, v], mean[:, v], half[:], ALU.pow).then_inc(S["rstd"], 1)

                def add(a):
                    pool.wait_ge(res_in[a.s], a.j * 16 + 16)
                    for g in range(G):
                        pool.wait_ge(S["gated"], a.n * 2 + (g + 1 + START))
                        if g == 0:
                            pool.wait_ge(S["out"], a.n - 1 + START)
                        cols = slice(g * GROUP, (g + 1) * GROUP)
                        nc.gpsimd.tensor_tensor(h3[:, a.s, cols], res[:, a.s, cols], gated[:, g],
                                                ALU.add).then_inc(S["h3"], 1)

                def root2(a):
                    v = slice(a.s, a.s + 1)
                    pool.wait_ge(S["mean2"], a.n + (1 + START))
                    nc.gpsimd.tensor_tensor(rstd2[:, v], mean2[:, v], half[:], ALU.pow).then_inc(S["rstd2"], 1)

                for name in "rstd h3 rstd2".split():
                    pool.sem_inc(S[name], START)
                nc.gpsimd.memset(half[:], -0.5).then_inc(half_set, 1)
                pool.wait_ge(half_set, 1)
                root(Tile(0, 0, 0))
                root(Tile(0, 0, 1))

                def pair(j, last):
                    for s in range(2):
                        a = Tile(j, j, s)
                        if not last:
                            root(a.next(2))
                        add(a)
                        root2(a)

                one_pass(pool, pair)

            @block.tensor
            def _(pe):
                def turn(a):
                    pe.wait_ge(S["hn"], a.n + (1 + START))
                    for b in range(2):
                        pe.wait_ge(S["lo"], a.n * 2 + (b - 1 + START))
                        for c in range(4):
                            ins = nc.tensor.transpose(turned[:, b, c * P:(c + 1) * P],
                                                      hn[:, a.s, (4 * b + c) * P:(4 * b + c + 1) * P], ident[:])
                        ins.then_inc(S["turn"], 1)
                    pe.wait_ge(emb_in[a.s], a.j * 16 + 16)
                    pe.wait_ge(S["e_lo"], a.n + START)
                    for c in range(PC):
                        ins = nc.tensor.transpose(e_turned[:, c * P:(c + 1) * P], emb[:, a.s, c * P:(c + 1) * P], ident[:])
                    ins.then_inc(S["e_turn"], 1)

                def products(a):
                    pe.wait_ge(S["lo"], a.n * 2 + (2 + START))
                    for g in range(G):
                        pe.wait_ge(S["w_lo"], g + 1 + START)
                        pe.wait_ge(S["gate"], a.n * 2 + (g - 1 + START))
                        for c in range(KC):
                            ins = matmul3(nc, gate_acc[:, g], xt_hi[:, a.s, c], xt_lo[:, a.s, c],
                                          w_hi[:, g, c], w_lo[:, g, c], c == 0, c == KC - 1)
                        ins.then_inc(S["gate_acc"], 1)
                    pe.wait_ge(S["e_wlo"], 1 + START)
                    pe.wait_ge(S["e_lo"], a.n + (1 + START))
                    for g in range(G):
                        pe.wait_ge(S["gated"], a.n * 2 + (g - 1 + START))
                        cols = slice(g * GROUP, (g + 1) * GROUP)
                        for c in range(PC):
                            ins = matmul3(nc, emb_acc[:, g], et_hi[:, a.s, c], et_lo[:, a.s, c],
                                          e_hi[:, c, cols], e_lo[:, c, cols], c == 0, c == PC - 1)
                        ins.then_inc(S["emb_acc"], 1)

                for name in "turn e_turn gate_acc emb_acc".split():
                    pe.sem_inc(S[name], START)
                pe.wait_ge(const_in, 48)
                turn(Tile(0, 0, 0))

                def pair(j, last):
                    for s in range(2):
                        a = Tile(j, j, s)
                        if not (last and s == 1):
                            turn(a.next(1))
                        products(a)

                one_pass(pe, pair)


PHASES = (project_phase, differential_phase, dilated_phase, mix_phase, mlp_phase, gate_phase)


def build(nc, dram):
    for phase in PHASES:
        kit = Kit(nc, dram)
        phase(kit)
        nc.all_engine_barrier()
        nc.clear_and_free_semaphores(kit.sems)
        nc.all_engine_barrier()



def shape_constants():
    inv = (10000.0 ** (-np.arange(0, HD, 2) / HD)).astype(np.float32)
    ang = np.arange(SEQ, dtype=np.float32)[:, None] * inv[None, :]
    cos, sin = np.cos(ang).astype(np.float32), np.sin(ang).astype(np.float32)
    rot = np.stack([np.concatenate([cos, cos], 1), np.concatenate([-sin, sin], 1)], 1)
    q, i = np.arange(P)[:, None], np.arange(2 * P)[None, :]
    near = np.abs(i - RADIUS - q) <= RADIUS
    kinds = (near & (i >= RADIUS), near, near & (i < P + RADIUS),
             near & (i >= RADIUS) & (i < P + RADIUS))
    masks = np.where(np.stack(kinds, 1), 0.0, NEG)
    return {"masks": np.ascontiguousarray(masks, np.float32), "rot": np.ascontiguousarray(rot, np.float32), "ident": np.eye(P, dtype=np.float32)}


INPUTS = {
    "x": (SEQ, DM), "p": (SEQ, D_PLE), "w_in": (DM, 6 * GROUP), "w_out": (DM, DM), "g_mix": (DM,),
    "lambda_q1": (1, HD), "lambda_k1": (1, HD), "lambda_q2": (1, HD), "lambda_k2": (1, HD),
    "g_subln": (2 * HD,), "g_mlp": (DM,), "w_up": (DM, D_FF), "w_down": (D_FF, DM), "g_ple": (DM,),
    "w_ple_gate": (DM, DM), "w_ple_proj": (D_PLE, DM), "g_final": (DM,),
}


def kernel(**inputs):
    import concourse.bacc as bacc
    from concourse.bass_utils import run_bass_kernel_spmd

    nc = bacc.Bacc("TRN2", target_bir_lowering=False, num_devices=1)
    arrays, dram = {}, {}
    for name, shape in INPUTS.items():
        arrays[name + "_dram"] = np.ascontiguousarray(np.asarray(inputs[name]).reshape(shape))
    for name, a in shape_constants().items():
        arrays[name + "_dram"] = a
    for name, a in arrays.items():
        dram[name[:-5]] = nc.dram_tensor(name, a.shape, F32, kind="ExternalInput").ap()
    dram["out"] = nc.dram_tensor("out_dram", (SEQ, DM), F32, kind="ExternalOutput").ap()
    for name, shape, dt in [
        ("qk", (2, 2, SEQ, MAPS, 2, HD), F32),
        ("v", (2, SEQ, 2 * GROUP), F32),
        ("od", (SEQ, GROUP), F32),
        ("nd", (len(PATTERNS), SEQ, MAPS, HD), F32),
        ("md", (len(PATTERNS), SEQ, MAPS, 2), F32),
        ("h", (SEQ, DM), F32),
        ("h2", (SEQ, DM), F32),
        ("xt", (TILES, P, KC, P), F32),
    ]:
        dram[name] = nc.dram_tensor("s_" + name, shape, dt).ap()
    build(nc, dram)
    result = run_bass_kernel_spmd(nc, [arrays], core_ids=[0])
    return result.results[0]["out_dram"].reshape(1, SEQ, DM)
```
